# Optimizing a Trainium2 kernel written in Bass

```python
import math
import jax, jax.numpy as jnp
from jax import lax
import numpy as np

D_MODEL = 1024
BATCH = 1
SEQ = 128
DEPTH = 2
DEC_BATCH = 1
DEC_SEQ = 256
PAST_LEN = 128

GRID_W = 64
EPS = 1e-6
NEG_INF = -1e30
CONV_W = 5
CHUNK = 64

SSD_HEADS = 4
SSD_HEAD_DIM = 64
SSD_WIDTH = SSD_HEADS * SSD_HEAD_DIM
SSD_GROUPS = 2
SSD_STATE = 64
SSD_CONV_CH = SSD_WIDTH + 2 * SSD_GROUPS * SSD_STATE
SSD_COLS = SSD_WIDTH + SSD_CONV_CH + 2 * SSD_HEADS
GDN_HEADS = 4
GDN_HEAD_DIM = 64
GDN_WIDTH = GDN_HEADS * GDN_HEAD_DIM
GDN_COLS = 4 * GDN_WIDTH + 4 * GDN_HEADS
FNET_GROUPS = 4
FNET_GROUP_DIM = 64
FNET_WIDTH = FNET_GROUPS * FNET_GROUP_DIM
FNET_COLS = FNET_WIDTH
ATT_HEADS = 4
ATT_KV_HEADS = 2
ATT_REP = ATT_HEADS // ATT_KV_HEADS
ATT_HEAD_DIM = 64
ATT_WIDTH = ATT_HEADS * ATT_HEAD_DIM
ATT_COLS = ATT_WIDTH + 2 * ATT_KV_HEADS * ATT_HEAD_DIM
WINDOW = 128
ABLOCK = 128
ROPE_THETA = 10000.0

MIX_WIDTH = SSD_WIDTH + GDN_WIDTH + FNET_WIDTH + ATT_WIDTH
IN_COLS = SSD_COLS + GDN_COLS + FNET_COLS + ATT_COLS

PEER_HEADS = 8
PEER_NKEYS = 128
PEER_EXPERTS = PEER_NKEYS * PEER_NKEYS
PEER_QDIM = 256
PEER_TOPK = 16
PEER_TOKEN_BLOCK = 128

kernel_name = 'hybrid_diffusion_peer_trunk_step'

def rmsnorm(x, w):
    xf = x.astype(jnp.float32)
    y = xf * lax.rsqrt(jnp.mean(xf * xf, axis=-1, keepdims=True) + EPS)
    return (y * w.astype(jnp.float32)).astype(x.dtype)

def l2norm(x):
    return x * lax.rsqrt(jnp.sum(x * x, axis=-1, keepdims=True) + EPS)

def adaln(cvec, w_mod, b_mod):
    m = jax.nn.silu(cvec) @ w_mod + b_mod
    return jnp.split(m[:, None, :], 6, axis=-1)

def dwconv_centred(x, w, b):
    ch = x.shape[-1]
    pad = (CONV_W - 1) // 2
    y = lax.conv_general_dilated(x, w[:, None, :].astype(x.dtype), window_strides=(1,),
                                 padding=[(pad, pad)], dimension_numbers=('NWC', 'WIO', 'NWC'),
                                 feature_group_count=ch)
    return y + b.astype(x.dtype)

def ssd_scan(x, dt, A, Bm, Cm, h0):
    b, l, h, p = x.shape
    n = Bm.shape[-1]
    nc = l // CHUNK
    a_cum = jnp.cumsum((dt * A).reshape(b, nc, CHUNK, h), axis=2)
    xdt = (x * dt[..., None]).reshape(b, nc, CHUNK, h, p)
    Bc = Bm.reshape(b, nc, CHUNK, h, n)
    Cc = Cm.reshape(b, nc, CHUNK, h, n)
    tri = jnp.tril(jnp.ones((CHUNK, CHUNK), dtype=bool))[:, :, None]
    seg = a_cum[:, :, :, None, :] - a_cum[:, :, None, :, :]
    Lmat = jnp.where(tri, jnp.exp(jnp.where(tri, seg, 0.0)), 0.0)
    y_diag = jnp.einsum('bcqhn,bckhn,bcqkh,bckhp->bcqhp', Cc, Bc, Lmat, xdt)
    decay_to_end = jnp.exp(a_cum[:, :, -1:, :] - a_cum)
    chunk_states = jnp.einsum('bckhn,bckh,bckhp->bchpn', Bc, decay_to_end, xdt)
    chunk_decay = jnp.exp(a_cum[:, :, -1, :])

    def step(state, inp):
        st, dec = inp
        return state * dec[:, :, None, None] + st, state

    h_final, h_enter = lax.scan(step, h0, (jnp.moveaxis(chunk_states, 1, 0),
                                           jnp.moveaxis(chunk_decay, 1, 0)))
    h_enter = jnp.moveaxis(h_enter, 0, 1)
    y_off = jnp.einsum('bcqhn,bchpn,bcqh->bcqhp', Cc, h_enter, jnp.exp(a_cum))
    return (y_diag + y_off).reshape(b, l, h, p), h_final

def ssd_mixer(u, conv_w, conv_b, A_log, dt_bias, D_skip, norm_w, h0):
    b, l, _ = u.shape
    f32 = jnp.float32
    z, xbc, dt_raw = jnp.split(u, [SSD_WIDTH, SSD_WIDTH + SSD_CONV_CH], axis=-1)
    xbc = jax.nn.silu(dwconv_centred(xbc, conv_w, conv_b)).astype(f32)
    xs, Bm, Cm = jnp.split(xbc, [SSD_WIDTH, SSD_WIDTH + SSD_GROUPS * SSD_STATE], axis=-1)
    xs = xs.reshape(b, l, SSD_HEADS, SSD_HEAD_DIM)
    rep = SSD_HEADS // SSD_GROUPS
    Bm = jnp.repeat(Bm.reshape(b, l, SSD_GROUPS, SSD_STATE), rep, axis=2)
    Cm = jnp.repeat(Cm.reshape(b, l, SSD_GROUPS, SSD_STATE), rep, axis=2)
    dt = jax.nn.softplus(dt_raw.astype(f32).reshape(b, l, 2, SSD_HEADS) + dt_bias.astype(f32))
    A = -jnp.exp(A_log.astype(f32))
    h0 = h0.astype(f32)
    y_f, h_f = ssd_scan(xs, dt[:, :, 0], A[0], Bm, Cm, h0[:, 0])
    y_b, h_b = ssd_scan(xs[:, ::-1], dt[:, ::-1, 1], A[1], Bm[:, ::-1], Cm[:, ::-1], h0[:, 1])
    y = y_f + y_b[:, ::-1] + D_skip.astype(f32)[:, None] * xs
    y = y * jax.nn.silu(z.astype(f32)).reshape(b, l, SSD_HEADS, SSD_HEAD_DIM)
    y = rmsnorm(y, norm_w.reshape(SSD_HEADS, SSD_HEAD_DIM))
    return y.reshape(b, l, SSD_WIDTH).astype(u.dtype), jnp.stack([h_f, h_b], axis=1)

def gdn_scan(q, k, v, log_alpha, beta, S0):
    b, l, h, dk = q.shape
    dv = v.shape[-1]
    nc = l // CHUNK

    def chunked(t):
        return jnp.moveaxis(t.reshape((b, nc, CHUNK) + t.shape[2:]), 2, 3)

    qc = chunked(q) * (dk ** -0.5)
    kc, vc = chunked(k), chunked(v)
    gcum = jnp.cumsum(chunked(log_alpha), axis=-1)
    bc = chunked(beta)
    tri = jnp.tril(jnp.ones((CHUNK, CHUNK), dtype=bool))
    strict = jnp.tril(jnp.ones((CHUNK, CHUNK), dtype=bool), k=-1)
    seg = gcum[..., :, None] - gcum[..., None, :]
    decay = jnp.where(tri, jnp.exp(jnp.where(tri, seg, 0.0)), 0.0)
    kk = jnp.einsum('bchid,bchjd->bchij', kc, kc)
    A = jnp.where(strict, bc[..., :, None] * kk * decay, 0.0)
    rhs = jnp.concatenate([vc * bc[..., None], kc * (bc * jnp.exp(gcum))[..., None]], axis=-1)
    sol = lax.linalg.triangular_solve(jnp.eye(CHUNK, dtype=A.dtype) + A, rhs,
                                      left_side=True, lower=True)
    u_c, w_c = sol[..., :dv], sol[..., dv:]
    attn = jnp.where(tri, jnp.einsum('bchid,bchjd->bchij', qc, kc) * decay, 0.0)
    q_dec = qc * jnp.exp(gcum)[..., None]
    k_end = kc * jnp.exp(gcum[..., -1:] - gcum)[..., None]
    c_dec = jnp.exp(gcum[..., -1])

    def step(S, inp):
        u_i, w_i, a_i, qd_i, ke_i, d_i = inp
        v_new = u_i - jnp.einsum('bhqk,bhkv->bhqv', w_i, S)
        o = jnp.einsum('bhqk,bhkv->bhqv', qd_i, S) + jnp.einsum('bhij,bhjv->bhiv', a_i, v_new)
        S = S * d_i[..., None, None] + jnp.einsum('bhqk,bhqv->bhkv', ke_i, v_new)
        return S, o

    xs = tuple(jnp.moveaxis(t, 1, 0) for t in (u_c, w_c, attn, q_dec, k_end, c_dec))
    S_final, o = lax.scan(step, S0, xs)
    o = jnp.transpose(o, (1, 0, 3, 2, 4)).reshape(b, l, h, dv)
    return o, S_final

def gdn_mixer(u, conv_w, conv_b, A_log, dt_bias, norm_w, S0):
    b, l, _ = u.shape
    f32 = jnp.float32
    qkv, gate, a_raw, b_raw = jnp.split(
        u, [3 * GDN_WIDTH, 4 * GDN_WIDTH, 4 * GDN_WIDTH + 2 * GDN_HEADS], axis=-1)
    qkv = jax.nn.silu(dwconv_centred(qkv, conv_w, conv_b)).astype(f32)
    q, k, v = [t.reshape(b, l, GDN_HEADS, GDN_HEAD_DIM) for t in jnp.split(qkv, 3, axis=-1)]
    q, k = l2norm(q), l2norm(k)
    log_alpha = -jnp.exp(A_log.astype(f32)) * jax.nn.softplus(
        a_raw.astype(f32).reshape(b, l, 2, GDN_HEADS) + dt_bias.astype(f32))
    beta = jax.nn.sigmoid(b_raw.astype(f32).reshape(b, l, 2, GDN_HEADS))
    S0 = S0.astype(f32)
    o_f, S_f = gdn_scan(q, k, v, log_alpha[:, :, 0], beta[:, :, 0], S0[:, 0])
    o_b, S_b = gdn_scan(q[:, ::-1], k[:, ::-1], v[:, ::-1], log_alpha[:, ::-1, 1],
                        beta[:, ::-1, 1], S0[:, 1])
    o = rmsnorm(o_f + o_b[:, ::-1], norm_w) * jax.nn.silu(gate.astype(f32)).reshape(
        b, l, GDN_HEADS, GDN_HEAD_DIM)
    return o.reshape(b, l, GDN_WIDTH).astype(u.dtype), jnp.stack([S_f, S_b], axis=1)

def fnet_mixer(u):
    b, l, _ = u.shape
    xf = u.astype(jnp.float32).reshape(b, l, FNET_GROUPS, FNET_GROUP_DIM)
    y = jnp.fft.fft2(xf, axes=(1, 3), norm='ortho').real
    return y.reshape(b, l, FNET_WIDTH).astype(u.dtype)

def axial_rope(l):
    rows = l // GRID_W
    row = jnp.repeat(jnp.arange(rows, dtype=jnp.float32), GRID_W)
    col = jnp.tile(jnp.arange(GRID_W, dtype=jnp.float32), rows)
    nf = ATT_HEAD_DIM // 4
    inv = ROPE_THETA ** (-jnp.arange(nf, dtype=jnp.float32) / nf)
    ang = jnp.concatenate([row[:, None] * inv, col[:, None] * inv], axis=-1)
    return jnp.cos(ang), jnp.sin(ang)

def apply_rope(x, cos, sin):
    half = ATT_HEAD_DIM // 2
    xf = x.astype(jnp.float32)
    x1, x2 = xf[..., :half], xf[..., half:]
    c, s = cos[None, :, None, :], sin[None, :, None, :]
    return jnp.concatenate([x1 * c - x2 * s, x2 * c + x1 * s], axis=-1).astype(x.dtype)

def sink_softmax(s, sink):
    sk = jnp.broadcast_to(sink[None, :, :, None, None], s.shape[:-1] + (1,))
    return jax.nn.softmax(jnp.concatenate([s, sk], axis=-1), axis=-1)[..., :-1]

def ctx_attention(q, k, v, sink):
    b, lc = q.shape[:2]
    nb = lc // ABLOCK
    scale = ATT_HEAD_DIM ** -0.5
    qb = q.astype(jnp.float32).reshape(b, nb, ABLOCK, ATT_KV_HEADS, ATT_REP, ATT_HEAD_DIM)
    kf, vf = k.astype(jnp.float32), v.astype(jnp.float32)
    sk = sink.astype(jnp.float32).reshape(ATT_KV_HEADS, ATT_REP)

    def one(qblk):
        s = jnp.einsum('bqgrd,bkgd->bgrqk', qblk, kf) * scale
        return jnp.einsum('bgrqk,bkgd->bqgrd', sink_softmax(s, sk), vf)

    o = lax.map(one, jnp.moveaxis(qb, 1, 0))
    return jnp.moveaxis(o, 0, 1).reshape(b, lc, ATT_WIDTH).astype(q.dtype)

def latent_attention(q, k, v, k_ctx, v_ctx, sink):
    b, l = q.shape[:2]
    nb = l // ABLOCK
    scale = ATT_HEAD_DIM ** -0.5
    f32 = jnp.float32
    qb = q.astype(f32).reshape(b, nb, ABLOCK, ATT_KV_HEADS, ATT_REP, ATT_HEAD_DIM)
    pad = ((0, 0), (ABLOCK, ABLOCK), (0, 0), (0, 0))
    kp, vp = jnp.pad(k.astype(f32), pad), jnp.pad(v.astype(f32), pad)
    kc, vc = k_ctx.astype(f32), v_ctx.astype(f32)
    sk = sink.astype(f32).reshape(ATT_KV_HEADS, ATT_REP)
    offs_q = jnp.arange(ABLOCK)
    offs_k = jnp.arange(3 * ABLOCK)

    def one(i):
        qblk = lax.dynamic_index_in_dim(qb, i, axis=1, keepdims=False)
        kl = lax.dynamic_slice_in_dim(kp, i * ABLOCK, 3 * ABLOCK, axis=1)
        vl = lax.dynamic_slice_in_dim(vp, i * ABLOCK, 3 * ABLOCK, axis=1)
        qpos = i * ABLOCK + offs_q
        kpos = (i - 1) * ABLOCK + offs_k
        ok = ((jnp.abs(qpos[:, None] - kpos[None, :]) <= WINDOW)
              & (kpos >= 0)[None, :] & (kpos < l)[None, :])
        s_loc = jnp.where(ok, jnp.einsum('bqgrd,bkgd->bgrqk', qblk, kl) * scale, NEG_INF)
        s_ctx = jnp.einsum('bqgrd,bkgd->bgrqk', qblk, kc) * scale
        pr = sink_softmax(jnp.concatenate([s_loc, s_ctx], axis=-1), sk)
        return (jnp.einsum('bgrqk,bkgd->bqgrd', pr[..., :3 * ABLOCK], vl)
                + jnp.einsum('bgrqk,bkgd->bqgrd', pr[..., 3 * ABLOCK:], vc))

    o = lax.map(one, jnp.arange(nb))
    return jnp.moveaxis(o, 0, 1).reshape(b, l, ATT_WIDTH).astype(q.dtype)

def peer(x, w_q, sub_keys, u_tab, v_tab):
    b, l, d = x.shape
    t = b * l
    f32 = jnp.float32
    xt = x.reshape(t, d)
    q = (xt @ w_q).astype(f32).reshape(t, PEER_HEADS, 2, PEER_QDIM // 2)
    s = jnp.einsum('thpc,hpkc->thpk', q, sub_keys.astype(f32))
    s_top, i_top = lax.top_k(s, PEER_TOPK)
    n_cand = PEER_TOPK * PEER_TOPK
    cand = (s_top[:, :, 0, :, None] + s_top[:, :, 1, None, :]).reshape(t, PEER_HEADS, n_cand)
    cand_idx = (i_top[:, :, 0, :, None] * PEER_NKEYS + i_top[:, :, 1, None, :]).reshape(
        t, PEER_HEADS, n_cand)
    best, pos = lax.top_k(cand, PEER_TOPK)
    idx = jnp.take_along_axis(cand_idx, pos, axis=-1).reshape(t, PEER_HEADS * PEER_TOPK)
    gate = jax.nn.softmax(best, axis=-1).reshape(t, PEER_HEADS * PEER_TOPK)
    nblk = t // PEER_TOKEN_BLOCK

    def block(args):
        xb, ib, gb = args
        act = jax.nn.gelu(jnp.einsum('ted,td->te', jnp.take(u_tab, ib, axis=0), xb).astype(f32),
                          approximate=False)
        w = (gb * act).astype(x.dtype)
        return jnp.einsum('te,ted->td', w, jnp.take(v_tab, ib, axis=0))

    out = lax.map(block, (xt.reshape(nblk, PEER_TOKEN_BLOCK, d),
                          idx.reshape(nblk, PEER_TOKEN_BLOCK, -1),
                          gate.reshape(nblk, PEER_TOKEN_BLOCK, -1)))
    return out.reshape(b, l, d)

def trunk_layer(x, mod, p, ssd_h0, gdn_h0, kv_ctx):
    sh1, sc1, g1, sh2, sc2, g2 = mod
    b, l, _ = x.shape
    h = rmsnorm(x, p['norm1_w']) * (1.0 + sc1) + sh1
    u = h @ p['w_in']
    u_ssd, u_gdn, u_fn, u_att = jnp.split(
        u, [SSD_COLS, SSD_COLS + GDN_COLS, SSD_COLS + GDN_COLS + FNET_COLS], axis=-1)
    y_ssd, ssd_state = ssd_mixer(u_ssd, p['ssd_conv_w'], p['ssd_conv_b'], p['ssd_A_log'],
                                 p['ssd_dt_bias'], p['ssd_D'], p['ssd_norm_w'], ssd_h0)
    y_gdn, gdn_state = gdn_mixer(u_gdn, p['gdn_conv_w'], p['gdn_conv_b'], p['gdn_A_log'],
                                 p['gdn_dt_bias'], p['gdn_norm_w'], gdn_h0)
    y_fn = fnet_mixer(u_fn)
    q, k, v = jnp.split(u_att, [ATT_WIDTH, ATT_WIDTH + ATT_KV_HEADS * ATT_HEAD_DIM], axis=-1)
    q = rmsnorm(q.reshape(b, l, ATT_HEADS, ATT_HEAD_DIM), p['q_norm_w'])
    k = rmsnorm(k.reshape(b, l, ATT_KV_HEADS, ATT_HEAD_DIM), p['k_norm_w'])
    v = v.reshape(b, l, ATT_KV_HEADS, ATT_HEAD_DIM)
    if kv_ctx is None:
        y_att = ctx_attention(q, k, v, p['att_sink'])
        kv_out = (k, v)
    else:
        cos, sin = axial_rope(l)
        y_att = latent_attention(apply_rope(q, cos, sin), apply_rope(k, cos, sin), v,
                                 kv_ctx[0], kv_ctx[1], p['att_sink'])
        kv_out = kv_ctx
    y = jnp.concatenate([y_ssd, y_gdn, y_fn, y_att], axis=-1) @ p['w_out']
    x = x + g1 * y
    h2 = rmsnorm(x, p['norm2_w']) * (1.0 + sc2) + sh2
    x = x + g2 * peer(h2, p['peer_w_q'], p['peer_keys'], p['peer_u'], p['peer_v'])
    return x, ssd_state, gdn_state, kv_out

def setup_inputs(seed: int = 0) -> dict:
    key = jax.random.key(seed)
    ks = iter(jax.random.split(key, 48))
    f32 = jnp.float32

    def nrm(shape, scale):
        return jax.random.normal(next(ks), shape, f32) * scale

    def gain(shape):
        return 1.0 + nrm(shape, 0.05)

    def dt_bias_init(shape):
        dt = jnp.exp(jax.random.uniform(next(ks), shape, f32, math.log(1e-3), math.log(1e-1)))
        return dt + jnp.log(-jnp.expm1(-dt))

    def a_log_init(shape):
        return jnp.log(jax.random.uniform(next(ks), shape, f32, 1.0, 16.0))

    return {
        'x_prompt': nrm((BATCH, SEQ, D_MODEL), 1.0),
        'x_sample': nrm((DEC_BATCH, DEC_SEQ, D_MODEL), 1.0),
        'cache_k': nrm((DEC_BATCH, DEPTH, PAST_LEN, ATT_KV_HEADS, ATT_HEAD_DIM), 1.0),
        'cache_v': nrm((DEC_BATCH, DEPTH, PAST_LEN, ATT_KV_HEADS, ATT_HEAD_DIM), 1.0),
        'state_ssd': nrm((DEC_BATCH, DEPTH, 2, SSD_HEADS, SSD_HEAD_DIM, SSD_STATE), 0.1),
        'state_gdn': nrm((DEC_BATCH, DEPTH, 2, GDN_HEADS, GDN_HEAD_DIM, GDN_HEAD_DIM), 0.1),
        'c': nrm((DEC_BATCH, D_MODEL), 1.0),
        'c_ctx': nrm((D_MODEL,), 1.0),
        'w_mod': nrm((DEPTH, D_MODEL, 6 * D_MODEL), 0.5 * D_MODEL ** -0.5),
        'b_mod': nrm((DEPTH, 6 * D_MODEL), 0.02),
        'norm1_w': gain((DEPTH, D_MODEL)),
        'norm2_w': gain((DEPTH, D_MODEL)),
        'w_in': nrm((DEPTH, D_MODEL, IN_COLS), D_MODEL ** -0.5),
        'w_out': nrm((DEPTH, MIX_WIDTH, D_MODEL), MIX_WIDTH ** -0.5),
        'ssd_conv_w': nrm((DEPTH, CONV_W, SSD_CONV_CH), CONV_W ** -0.5),
        'ssd_conv_b': nrm((DEPTH, SSD_CONV_CH), 0.02),
        'ssd_A_log': a_log_init((DEPTH, 2, SSD_HEADS)),
        'ssd_dt_bias': dt_bias_init((DEPTH, 2, SSD_HEADS)),
        'ssd_D': gain((DEPTH, SSD_HEADS)),
        'ssd_norm_w': gain((DEPTH, SSD_WIDTH)),
        'gdn_conv_w': nrm((DEPTH, CONV_W, 3 * GDN_WIDTH), CONV_W ** -0.5),
        'gdn_conv_b': nrm((DEPTH, 3 * GDN_WIDTH), 0.02),
        'gdn_A_log': a_log_init((DEPTH, 2, GDN_HEADS)),
        'gdn_dt_bias': dt_bias_init((DEPTH, 2, GDN_HEADS)),
        'gdn_norm_w': gain((DEPTH, GDN_HEAD_DIM)),
        'q_norm_w': gain((DEPTH, ATT_HEAD_DIM)),
        'k_norm_w': gain((DEPTH, ATT_HEAD_DIM)),
        'att_sink': nrm((DEPTH, ATT_HEADS), 0.5),
        'peer_w_q': nrm((DEPTH, D_MODEL, PEER_HEADS * PEER_QDIM), D_MODEL ** -0.5),
        'peer_keys': nrm((DEPTH, PEER_HEADS, 2, PEER_NKEYS, PEER_QDIM // 2), (PEER_QDIM // 2) ** -0.5),
        'peer_u': nrm((DEPTH, PEER_EXPERTS, D_MODEL), D_MODEL ** -0.5),
        'peer_v': nrm((DEPTH, PEER_EXPERTS, D_MODEL), 0.5),
    }

def reference(x_prompt, x_sample, cache_k, cache_v, state_ssd, state_gdn, c, c_ctx,
              w_mod, b_mod, norm1_w, norm2_w, w_in, w_out,
              ssd_conv_w, ssd_conv_b, ssd_A_log, ssd_dt_bias, ssd_D, ssd_norm_w,
              gdn_conv_w, gdn_conv_b, gdn_A_log, gdn_dt_bias, gdn_norm_w,
              q_norm_w, k_norm_w, att_sink, peer_w_q, peer_keys, peer_u, peer_v):
    stacked = dict(w_mod=w_mod, b_mod=b_mod, norm1_w=norm1_w, norm2_w=norm2_w, w_in=w_in,
                   w_out=w_out, ssd_conv_w=ssd_conv_w, ssd_conv_b=ssd_conv_b,
                   ssd_A_log=ssd_A_log, ssd_dt_bias=ssd_dt_bias, ssd_D=ssd_D,
                   ssd_norm_w=ssd_norm_w, gdn_conv_w=gdn_conv_w, gdn_conv_b=gdn_conv_b,
                   gdn_A_log=gdn_A_log, gdn_dt_bias=gdn_dt_bias, gdn_norm_w=gdn_norm_w,
                   q_norm_w=q_norm_w, k_norm_w=k_norm_w, att_sink=att_sink,
                   peer_w_q=peer_w_q, peer_keys=peer_keys, peer_u=peer_u, peer_v=peer_v)
    bp = x_prompt.shape[0]
    zeros_ssd = jnp.zeros((bp, 2, SSD_HEADS, SSD_HEAD_DIM, SSD_STATE), jnp.float32)
    zeros_gdn = jnp.zeros((bp, 2, GDN_HEADS, GDN_HEAD_DIM, GDN_HEAD_DIM), jnp.float32)

    xp = x_prompt
    ks, vs, ssd_states, gdn_states = [], [], [], []
    for i in range(DEPTH):
        p = {name: arr[i] for name, arr in stacked.items()}
        mod = adaln(c_ctx[None, :], p['w_mod'], p['b_mod'])
        xp, s_ssd, s_gdn, kv = trunk_layer(xp, mod, p, zeros_ssd, zeros_gdn, None)
        ks.append(kv[0])
        vs.append(kv[1])
        ssd_states.append(s_ssd)
        gdn_states.append(s_gdn)
    new_cache_k = jnp.stack(ks, axis=1).astype(x_prompt.dtype)
    new_cache_v = jnp.stack(vs, axis=1).astype(x_prompt.dtype)
    new_state_ssd = jnp.stack(ssd_states, axis=1).astype(x_prompt.dtype)
    new_state_gdn = jnp.stack(gdn_states, axis=1).astype(x_prompt.dtype)

    xs = x_sample
    for i in range(DEPTH):
        p = {name: arr[i] for name, arr in stacked.items()}
        mod = adaln(c, p['w_mod'], p['b_mod'])
        xs, _, _, _ = trunk_layer(xs, mod, p, state_ssd[:, i], state_gdn[:, i],
                                  (cache_k[:, i], cache_v[:, i]))

    return (xp, xs, new_cache_k, new_cache_v, new_state_ssd, new_state_gdn)


_drawn_inputs = setup_inputs


def setup_inputs(seed=0):
    import zlib

    import numpy as np

    out = dict(_drawn_inputs(seed))
    spreads = {}
    factors = {'cache_k': 3.941,
     'cache_v': 3.424,
     'state_gdn': 2.943,
     'ssd_D': 7.166,
     'ssd_norm_w': 3.994,
     'gdn_norm_w': 5.315,
     'q_norm_w': 8.0,
     'att_sink': 8.0}
    for name, (base, spread) in spreads.items():
        noise = np.random.default_rng([zlib.crc32(name.encode()), seed]).standard_normal(out[name].shape)
        drawn = base * np.exp(spread * noise) if base else spread * noise
        out[name] = __import__('jax').numpy.asarray(drawn.astype(out[name].dtype))
    for name, factor in factors.items():
        out[name] = (out[name] * factor).astype(out[name].dtype)
    return out
```

```python
from contextlib import ExitStack, nullcontext

import numpy as np

import concourse.bass as bass
from concourse import mybir

F32 = mybir.dt.float32
U32 = mybir.dt.uint32
ALU = mybir.AluOpType
ACT = mybir.ActivationFunctionType
AX_X = mybir.AxisListType.X

P = 128
D = 1024
DC = D // P
DEPTH = 2
EPS = 1e-6
NEG = -1e30
IN_COLS = 2584
HEADS = 4
HD = 64
CONV_W = 5
LEVELS = 7
PH = 8
TOPK = 16
NKEYS = 128
SLOTS = PH * TOPK
GRID_W = 64
ROPE_THETA = 10000.0

Z0, XBC0, DT0, QKV0, GATE0, AB0, FN0, ATT0 = 0, 256, 768, 776, 1544, 1800, 1816, 2072

GROUP_TILES = [[0], [1, 2]]
UNITS = [(0, 0), (1, 0), (0, 1), (1, 1)]

HB = 4
STEP = 2 * HB
STEPS = SLOTS // STEP
PE_SLOTS = 3
FREE_SLOTS = 2
SLOTS_BESIDE = {"proj": 1, "intra0": 1, "intra1": 1, "out": 1, "query": 1, "topk0": 3, "topk1": 3}
WB = 256
WRING = 2


def seq_tiles(u):
    first = [0, 1, 3, 4][u]
    return [(first + i, t) for i, t in enumerate(GROUP_TILES[UNITS[u][0]])]


def constants():
    i = np.arange(P)
    parts = {}
    parts["ident"] = np.eye(P)
    parts["ones"] = np.ones((P, P))
    parts["tri"] = np.concatenate([i[:, None] <= i[None, :], i[:, None] >= i[None, :]], 1)
    parts["negm"] = np.concatenate([np.where(i[:, None] <= i[None, :], 0, NEG), np.where(i[:, None] >= i[None, :], 0, NEG)], 1)
    lv = []
    for flip in (0, 1):
        for l in range(LEVELS):
            same = (i[:, None] >> (l + 1)) == (i[None, :] >> (l + 1))
            m = same & (((i[:, None] >> l) & 1) == 0) & (((i[None, :] >> l) & 1) == 1)
            lv.append(m.T if flip else m)
    levels = np.concatenate(lv, 1).astype(np.float32)
    c = np.arange(HD)
    ch = 2 * np.pi * np.outer(c, c) / HD
    chan = np.zeros((P, 2, P))
    for b in (0, 1):
        chan[64 * b:64 * b + 64, 0, 64 * b:64 * b + 64] = np.cos(ch)
        chan[64 * b:64 * b + 64, 1, 64 * b:64 * b + 64] = np.sin(ch)
    parts["chan"] = chan.reshape(P, -1)
    for name, L in (("dftP", 128), ("dftS", 256)):
        k = np.arange(L)
        a = 2 * np.pi * (np.outer(k, k) % L) / L
        cs = np.stack([np.cos(a), -np.sin(a)], 0) / np.sqrt(L * HD)
        parts[name] = cs.reshape(2, L // P, P, L).transpose(2, 1, 0, 3).reshape(P, -1)
    blk = np.zeros((P, P))
    blk[:64, :64] = 1
    blk[64:, 64:] = 1
    parts["blk"] = blk
    pos = np.arange(256)
    row, col = (pos // GRID_W).astype(np.float64), (pos % GRID_W).astype(np.float64)
    inv = ROPE_THETA ** (-np.arange(HD // 4) / (HD // 4))
    ang = np.concatenate([row[:, None] * inv, col[:, None] * inv], -1)
    rope = np.stack([np.cos(ang), np.sin(ang)], 1)
    parts["rope"] = rope.reshape(2, P, 2, 32).transpose(1, 0, 2, 3).reshape(P, -1)
    dist = np.abs(np.arange(256)[:, None] - np.arange(256)[None, :])
    wm = np.where(dist <= 128, 0, NEG)
    parts["wmask"] = wm.reshape(2, P, 256).transpose(1, 0, 2).reshape(P, -1)
    parts["iota16"] = np.tile(np.arange(16), (P, 1))
    where, at = {}, 0
    for n, a in parts.items():
        where[n] = (at, a.shape[1])
        at += a.shape[1]
    return np.concatenate([a.astype(np.float32) for a in parts.values()], 1), where, levels


def mix_points(u):
    g, nt = UNITS[u][0], len(GROUP_TILES[UNITS[u][0]])
    pts = []

    def add(stage, inner, w, end=0):
        pts.extend(((stage, k), w) for k in inner)
        pts.append((stage, end))

    if u == 2:
        add("mod", range(24), 8)
    add("load", [], 0)
    add("norm1", [0], 3, 5)
    add("proj", range(16), 3 * nt, 3)
    add("scal", [0, 1], 4, 4)
    add("pre", [0], 3, 5)
    for i in range(nt):
        add(f"intra{i}", [0, 1, 2, 3, 4, 5, 6, 7, 8, 9], 5, 3)
    add("scan", range(8) if g else [6, 7], 5, 5)
    add("fnet", [], 1, 5)
    add("attp", [0], 4, 5)
    for i in range(nt):
        add(f"att{i}", range(3), 4, 3)
    add("out", range(8), 2 * nt, 2)
    add("query", range(17), 2 * nt, 4)
    for i in range(nt):
        add(f"topk{i}", range(10), 4, 4)
    return pts


def stages_of(u):
    return [k for k, _ in mix_points(u) if isinstance(k, str)]


def schedule():
    main = [("const",), ("modcols", 0)]
    side, upto = [], {}
    for u in range(len(UNITS)):
        if u == 0:
            own = [("modblocks", 0, k, k + 1) for k in range(8, 24)] + [("modsum", 0, 1)]
        else:
            own = []
            for q, t in seq_tiles(u - 1):
                own += [("u", q, t, i, i + 1, (h,)) for i in range(STEPS) for h in range(2)]
            for q, t in seq_tiles(u - 1):
                own += [("gelu", q, t)] + [("v", q, t, i, i + 1, (h,)) for i in range(STEPS) for h in range(2)] + [("end", u - 1, q, t)]
        pts, beside = mix_points(u), []
        if u == 0:
            first, last = [n for n, (k, _) in enumerate(pts) if k in ("proj", "att0")]
            pts = [(k, w if first < n <= last else 0) for n, (k, w) in enumerate(pts)]
        total, steps, past, n = sum(w for _, w in pts), sum(it[0] in ("u", "v", "modblocks") for it in own), 0, 0
        for k, w in pts:
            past += w
            ran = sum(it[0] in ("u", "v", "modblocks") for it in own[:n])
            while n < len(own) and (own[n][0] not in ("u", "v", "modblocks") or ran + 1 <= past / total * steps + 1e-6):
                if own[n][0] in ("gelu", "end", "modsum") and not isinstance(k, str):
                    break
                ran += own[n][0] in ("u", "v", "modblocks")
                n += 1
            upto[u, k] = len(side) + n
            beside += [SLOTS_BESIDE.get(k if isinstance(k, str) else k[0], FREE_SLOTS)] * (n - len(beside))
        beside += [FREE_SLOTS] * (len(own) - len(beside))
        side += [it + (b,) if it[0] == "v" else it for it, b in zip(own, beside)]
        for st in stages_of(u):
            main.append(("mix", st, u))
            if (st, u) == ("load", 0):
                main += [("modblocks", 0, 0, 8), ("modsum", 0, 0)]
        main.append(("drain", u))
        upto[u, "drain"] = len(side)
    for q, t in seq_tiles(3):
        main.append(("u", q, t, 0, STEPS, (0, 1)))
    for q, t in seq_tiles(3):
        main += [("gelu", q, t), ("v", q, t, 0, STEPS, (0, 1), FREE_SLOTS), ("end", 3, q, t)]
    main.append(("final",))
    return main, side, upto


SHARED = {
    "setup_full": ["cols_full", "keys_full", "x_full_", "mod_full"],
    "proj_banks_full": ["proj_full", "tokcols_full", "raw_full"],
    "prep_banks_full": ["sums_full", "l2_full", "xB_full", "kv_full"],
    "chunk_banks_full": ["rows_full", "cb_full", "kk_full", "qk_full", "beta_full", "y_full"],
    "inverse_full": ["x_full", "p_full", "xt_full", "u_full", "wt_full"],
    "scan_banks_full": ["ssd_state_full", "gdn_state_full", "h_loaded_full", "yoff_full", "w_full", "qs_full", "dh_full",
                        "ds_full", "o_full"],
    "mix_banks_full": ["xcs_full", "fnet_full", "qkT_full", "kcT_full", "scores_full", "pT_full", "att_full", "y_full_T"],
    "tail_banks_full": ["out_full", "rms_full", "h2_full", "q_full", "s_full", "acc_full", "v_full", "x_out_full"],
    "setup_copied": ["c_silu", "cols_copied", "keys_copied", "x_copied_", "x_out_copied"],
    "proj_kept": ["proj_copied", "silu_done", "tokcols_copied", "raw_copied"],
    "act_scalars": ["exp_neg", "sums_copied", "decays", "qk_squares", "l2_read", "xB_copied", "kv_copied"],
    "act_chunk": ["x0_ready", "dec_ready", "p_copied", "u_copied", "wt_copied"],
    "act_scan": ["ssd_out", "gdn_out", "h_loaded", "ms_roots"],
    "act_mix": ["xcs_copied", "fnet_copied", "att_roots", "qkT_copied", "kcT_copied", "probs_ready", "sink_ready",
                "pT_copied", "yT_copied"],
    "act_tail": ["squares", "rms_read", "h_ready", "h2_copied", "q_copied", "s_copied", "gate_exp", "gelu_done"],
    "dve_setup": ["init", "mod_copied", "modA_ready"],
    "dve_scalars": ["neg_abs", "lat_ready", "to_end", "qk_normed", "h_normed", "conv_done"],
    "dve_chunk": ["summands_ready", "beta_diag", "rows_read", "cb_read", "m_ready", "qk_read", "kk_read", "n_ready",
                  "y_read", "rhs_ready", "intra_done"],
    "dve_inverse": ["x_ready", "noff_ready", "xt_ready"],
    "dve_scan": ["yoff_read", "v_ready", "qs_read", "h_updated", "state_ready", "o_read", "ms_ready"],
    "dve_mix": ["att_ms", "qk_rows", "scores_read", "max_ready", "att_read", "ycat_ready"],
    "dve_tail": ["x_added", "best_shifted", "idx_ready", "mix_done", "dots_done", "w_ready", "v_summed", "x_added2"],
}
SEMAPHORE_OF = {m: s for s, ms in SHARED.items() for m in ms}


def build(nc, a, outs, seen):
    noted, counts = {}, {}
    _, CW, _ = constants()
    sched, side, upto = schedule()
    phase_of, v_before = {}, {}
    for it in side + sched:
        if it[0] in ("u", "v") and it[:2] not in phase_of:
            v_before[it[:2]] = sum(k == "v" for k, _ in phase_of)
            phase_of[it[:2]] = len(phase_of)

    with ExitStack() as ctx:
        def sb(name, shape, dt=F32):
            return ctx.enter_context(nc.sbuf_tensor("sb_" + name, shape, dt))

        sems = {}

        def sem(name):
            if name not in sems:
                sems[name] = ctx.enter_context(nc.semaphore(name))
            return sems[name]

        def tick(name, key=0, by=1):
            s = SEMAPHORE_OF.get(name, name)
            counts[s] = counts.get(s, 0) + by
            noted[name, key] = counts[s]
            return sem(s), by

        def done(name, key=0):
            return sem(SEMAPHORE_OF.get(name, name)), seen[name, key] if seen else 1

        def stepper(name):
            def step():
                return tick(name)

            def stepped():
                return sem(name), counts[name]
            return step, stepped

        cst = sb("cst", [P, sum(w for _, w in CW.values())])

        def con(name, i=0, n=None):
            o, w = CW[name]
            n = w if n is None else n
            return cst[:, o + i * n:o + i * n + n]

        lvl = sb("lvl", [P, 2, LEVELS, P], mybir.dt.uint8)
        ident, ones, blk = con("ident"), con("ones"), con("blk")
        xT = sb("xT", [P, DC, 3 * P])
        hT = sb("hT", [P, DC, 2 * P])
        wring = sb("wring", [P, WRING, DC, WB])
        wsm = sb("wsm", [P, DC, 24])
        prm = sb("prm", [P, 488])
        cT = sb("cT", [P, 2, DC])
        modT = sb("modT", [P, DEPTH, 48, 2])
        modA = sb("modA", [P, DEPTH, 2, DC, 2])
        colT = sb("colT", [P, 64])
        convT = sb("convT", [P, 10, 6])
        keysT = sb("keysT", [P, 16, P])
        h2 = sb("h2", [P, 3, D])
        ring = sb("ring", [P, STEP, D])
        diag = sb("diag", [P, 2 * PE_SLOTS, P])
        accv = sb("accv", [P, D])
        idxu = sb("idxu", [P, 3, SLOTS], U32)
        idxc = sb("idxc", [P, STEP], U32)
        gatew = sb("gatew", [P, 3, SLOTS])
        dots = sb("dots", [P, 3, SLOTS])
        dot8 = sb("dot8", [P, STEP])
        zero = sb("zero", [P, P])
        epsc = sb("epsc", [P, 1])
        spare = sb("spare", [P, 4])
        cinP = sb("cinP", [P, 2, P + 4])
        cinS = sb("cinS", [P, 2, 2 * P + 4])
        cv = sb("cv", [P, 10, 2 * P])
        fnx = sb("fnx", [P, 2, 2 * P])
        zs = sb("zs", [P, 2, 2, 256])
        qkv = sb("qkv", [P, 2, 512])
        raw = sb("raw", [P, 2, 24])
        sca = sb("sca", [P, 12, 2, 24])
        lat = sb("lat", [P, 2, 16])
        spt = sb("spt", [P, 2, 16])
        bet = sb("bet", [P, 2, 8])
        gct = sb("gct", [P, 2, 32])
        ege = sb("ege", [P, 2, 32])
        dte = sb("dte", [P, 2, 16])
        dec = sb("dec", [P, 2, 8, P])
        ycat = dec[:, :, :, :].rearrange("p a b c -> p a (b c)")
        tok = sb("tok", [P, 2, 896])
        big = sb("big", [P, 5120])
        attnT = hT[:, :, :].rearrange("p a b -> p (a b)").rearrange("p (i d n) -> p i d n", i=2, d=2)
        sol = sb("sol", [P, 2, 2, 256])
        solW = sb("solW", [P, 2, 512])
        xe = sb("xe", [P, 2, 256])
        ke = sb("ke", [P, 2, 256])
        ydg = sb("ydg", [P, 2, 256])
        og = sb("og", [P, 2, 256])
        stn = sb("stn", [P, 256])
        hst = sb("hst", [P, 2, P])
        sgd = sb("sgd", [P, 2, 2, HD])
        kTt = solW[:, 0, 0:384].rearrange("p (a b) -> p a b", b=P)
        qTt = solW[:, 1, :].rearrange("p (i a b) -> p i a b", i=2, a=2)
        vc = sb("vc", [P, 2, P])
        sm = sb("sm", [P, 8, 8])
        v16 = xe[:, 0, :].rearrange("p (a b) -> p a b", b=16)
        i16u = sb("i16u", [P, 16, 16], U32)
        i16f = ke[:, 0, :].rearrange("p (a b) -> p a b", b=16)
        best = sb("best", [P, 8, 16])
        pos = sb("pos", [P, 3, SLOTS], U32)
        posf = sb("posf", [P, 2, SLOTS])
        hexp = sb("hexp", [P, 2, SLOTS])
        pb = ctx.enter_context(nc.psum_tensor("pb", [P, 6, 512], F32))
        pv = ctx.enter_context(nc.psum_tensor("pv", [P, 2, 512], F32))

        PRM = {"A": (0, 16), "bias": (16, 16), "D": (32, 4), "sink": (36, 4), "qn": (40, 64), "kn": (104, 64),
               "gn": (168, 64), "sn": (232, 256)}

        def pr(name):
            o, n = PRM[name]
            return prm[:, o:o + n]

        def bc1(ap, n):
            return ap.unsqueeze(1).to_broadcast((ap.shape[0], n) + tuple(ap.shape[1:]))

        def bc2(ap, n):
            return ap.unsqueeze(len(ap.shape)).to_broadcast(tuple(ap.shape) + (n,))

        def dims(u):
            g, l = UNITS[u]
            nt = len(GROUP_TILES[g])
            return g, l, nt, nt * P, g * P

        def heads_by_parity(ap):
            return ap.rearrange("p (pair par) n -> p par pair n", par=2)

        def big_at(o, *shape):
            n = int(np.prod(shape))
            v = big[:, o:o + n]
            if len(shape) == 2:
                return v.rearrange("p (a b) -> p a b", b=shape[1])
            if len(shape) == 3:
                return v.rearrange("p (a b c) -> p a b c", b=shape[1], c=shape[2])
            return v

        rows_in = [sem(f"rows_in{j}") for j in range(STEP)]
        used_dve = [sem(f"rows_used_dve{h}") for h in range(2)]
        used_pe = [sem(f"rows_used_pe{h}") for h in range(2)]
        diag_ready = [sem(f"diag_ready{h}") for h in range(2)]
        slot_added = sem("slot_added")
        idx_copied, spare_sem, dots_kept = sem("idx_copied"), sem("spare_step"), sem("dots_kept")

        def engine_schedule(items, stages):
            ran = [0]

            def gap(u, *point):
                point = point[0] if len(point) == 1 else point
                while ran[0] < upto[u, point]:
                    it = side[ran[0]]
                    ran[0] += 1
                    items.get(it[0], lambda *x: None)(*it[1:])

            def run():
                for it in sched:
                    if it[0] == "mix":
                        stages.get(it[1], lambda u: None)(it[2])
                        gap(it[2], it[1])
                    elif it[0] == "drain":
                        gap(it[1], "drain")
                    else:
                        items.get(it[0], lambda *x: None)(*it[1:])
            return gap, run

        def steps(eng, i0, i1):
            return eng.Fori(i0, i1) if i1 - i0 > 1 else nullcontext(i0)

        def mod_blocks(l, k0, k1):
            return [a["w_mod"][l, :, WB * k:WB * k + WB] for k in range(k0, k1)]

        blocks = mod_blocks(0, 0, 8)
        for it in sched:
            if it[0] == "mix":
                l = UNITS[it[2]][1]
                if it[1] == "mod":
                    blocks += mod_blocks(l, 0, 24)
                elif it[1] == "proj":
                    blocks += [a["w_in"][l, :, c:c + WB] for c in (XBC0, XBC0 + 256, QKV0, QKV0 + 256, QKV0 + 512, FN0,
                                                                  Z0, GATE0, ATT0, ATT0 + 256)]
                    if it[2] == 0:
                        blocks += mod_blocks(0, 8, 24)
                elif it[1] == "out":
                    blocks += [a["w_out"][l, :, WB * k:WB * k + WB] for k in range(4)]
                elif it[1] == "query":
                    blocks += [a["peer_w_q"][l, :, WB * k:WB * k + WB] for k in range(8)]

        def modps(l):
            return pb[:, 3, :] if l else pv[:, 0, :]

        block = ctx.enter_context(nc.Block())

        @block.sync
        def _(sp):
            nblk = [0]

            def load_blocks(n):
                for _ in range(n):
                    b = nblk[0]
                    if b >= WRING and seen:
                        sp.wait_ge(*done(*seen["last use of block", b - WRING]))
                    sp.dma_start(wring[:, b % WRING], blocks[b].rearrange("(c p) n -> p c n", p=P)) \
                        .then_inc(*tick(f"wblock_in{b % WRING}", b, 16))
                    nblk[0] += 1

            def small(dst, src, key):
                sp.dma_start(dst, src, allow_slow_non_contiguous=key[0] == "cT") \
                    .then_inc(*tick("small_in_" + key[0], key, 16))

            def item_const():
                small(cst[:, :], a["cst"], ("cst", 0))
                small(dec[:, :, :, :].rearrange("p a b c -> p (a b c)")[:, 0:2 * LEVELS * P], a["lvl"], ("cst", 1))
                small(cT[:, 0, :], a["c_ctx"].rearrange("(c p) -> p c", p=P), ("cT", 0))
                small(cT[:, 1, :], a["c"][0].rearrange("(c p) -> p c", p=P), ("cT", 1))

            def item_modcols(l):
                if l:
                    sp.wait_ge(*done("mix_done", 2 * l - 1))
                v = "(a n) -> a n"
                big_r = big[0:64, 1280:1408]
                small(big_r[0:48], a["b_mod"][l].rearrange(v, n=P), ("col", l, 0))
                small(big_r[48:56], a["norm1_w"][l].rearrange(v, n=P), ("col", l, 1))
                small(big_r[56:64], a["norm2_w"][l].rearrange(v, n=P), ("col", l, 2))
                small(big[0:5, 0:512], a["ssd_conv_w"][l], ("col", l, 3))
                small(big[0:5, 512:1280], a["gdn_conv_w"][l], ("col", l, 4))
                small(big[5:6, 0:512], a["ssd_conv_b"][l].rearrange(v, a=1), ("col", l, 5))
                small(big[5:6, 512:1280], a["gdn_conv_b"][l].rearrange(v, a=1), ("col", l, 6))
                small(big_at(1408, 16, P), a["peer_keys"][l].rearrange("h t k c -> k (h t) c"), ("col", l, 7))
                small(wsm[:, :, 0:8], a["w_in"][l, :, DT0:DT0 + 8].rearrange("(c p) n -> p c n", p=P), ("wsm", l, 0))
                small(wsm[:, :, 8:24], a["w_in"][l, :, AB0:AB0 + 16].rearrange("(c p) n -> p c n", p=P), ("wsm", l, 1))
                at = 0
                for name in ("ssd_A_log", "gdn_A_log", "ssd_dt_bias", "gdn_dt_bias", "ssd_D", "att_sink", "q_norm_w",
                             "k_norm_w", "gdn_norm_w", "ssd_norm_w"):
                    src = a[name][l]
                    if len(src.shape) == 2:
                        src = src.rearrange("a b -> (a b)")
                    n = src.shape[0]
                    small(prm[:, at:at + n], src.rearrange(v, a=1).to_broadcast((P, n)), ("prm", l, at))
                    at += n

            def item_mix(stage, u):
                g, l, nt, NC, c0 = dims(u)
                if stage == "load" and u:
                    sp.wait_ge(*done("mix_done", u - 1))
                elif stage == "load":
                    sp.wait_ge(*done("init"))
                if stage == "load" and l == 0:
                    for i in range(nt):
                        src = a["x_prompt"][0] if g == 0 else a["x_sample"][0, i * P:i * P + P, :]
                        small(ycat[:, i, :], src, ("x", u, i))
                if stage == "load" and g == 1:
                    for d in range(2):
                        small(stn[:, d * P:d * P + P].rearrange("q (g n) -> q g n", g=2)[0:64],
                              a["state_ssd"][0, l, d].rearrange("(g r) p n -> r p g n", r=2)[0], ("st", u, d, 0))
                        small(stn[:, d * P:d * P + P].rearrange("q (g n) -> q g n", g=2)[64:128],
                              a["state_ssd"][0, l, d].rearrange("(g r) p n -> r p g n", r=2)[1], ("st", u, d, 1))
                        for par in range(2):
                            small(sgd[64 * par:64 * par + 64, d],
                                  a["state_gdn"][0, l, d].rearrange("(pair par) k v -> par k pair v", par=2)[par],
                                  ("sgd", u, d, par))
                    small(vc[:, 0, :], a["cache_k"][0, l].rearrange("s h d -> s (h d)"), ("vc", u, 0))
                    small(vc[:, 1, :], a["cache_v"][0, l].rearrange("s h d -> s (h d)"), ("vc", u, 1))
                if stage == "mod":
                    item_modcols(l)
                load_blocks({"mod": 24, "proj": 10 if u else 26, "out": 4, "query": 8}.get(stage, 0))

            def item_modblocks(l, k0, k1):
                load_blocks(k1 - k0)

            for it in sched:
                {"const": item_const, "modcols": item_modcols, "modblocks": item_modblocks,
                 "mix": item_mix}.get(it[0], lambda *x: None)(*it[1:])

        @block.gpsimd
        def _(pool):
            def item_u(q, t, i0, i1, kind="u"):
                p = phase_of[kind, q]
                nv = v_before[kind, q]
                if i0 == 0:
                    pool.wait_ge(*done("idx_ready", q))
                with pool.Fori(i0, i1) as i:
                    for h in range(2):
                        pool.wait_ge(used_dve[h], i + (p * STEPS + 1))
                        if kind == "v":
                            pool.wait_ge(used_pe[h], i + (nv * STEPS + 1))
                        elif nv:
                            pool.wait_ge(used_pe[h], nv * STEPS + 1)
                        pool.tensor_copy(idxc[:, h * HB:h * HB + HB],
                                         idxu[:, t, bass.ds(i * STEP + h * HB, HB)]).then_inc(idx_copied, 1)
                        pool.wait_ge(idx_copied, i * 4 + (p * STEPS * 4 + h * 2 + 1))
                        pool.tensor_tensor(spare[:, 2:3], spare[:, 0:1], spare[:, 0:1], ALU.add).then_inc(idx_copied, 1)
                        for j in range(h * HB, h * HB + HB):
                            pool.indirect_dma_start(ring[:, j, :], None, a["tab_" + kind][l_of(q)],
                                                    bass.IndirectOffsetOnAxis(ap=idxc[:, j:j + 1], axis=0)
                                                    ).then_inc(rows_in[j], 16)

            def l_of(q):
                return 0 if q < 3 else 1

            pool.memset(spare[:, :], 0.0).then_inc(spare_sem, 1)
            pool.wait_ge(spare_sem, 1)
            for kind, q in phase_of:
                t = [t for u in range(4) for qq, t in seq_tiles(u) if qq == q][0]
                item_u(q, t, 0, STEPS, kind)

        @block.tensor
        def _(pe):
            held = {}
            nblk = [0]

            def take(banks, until):
                for b in banks:
                    if b in held:
                        pe.wait_ge(*done(*held[b]))
                    held[b] = until

            def mm(out, lhsT, rhs, start=True, stop=True):
                return nc.tensor.matmul(out, lhsT, rhs, start=start, stop=stop)

            def tr(out, in_):
                return nc.tensor.transpose(out, in_, ident[0:in_.shape[0], 0:in_.shape[0]])

            def next_block():
                b = nblk[0]
                pe.wait_ge(*done(f"wblock_in{b % WRING}", b))
                nblk[0] += 1
                return b, wring[:, b % WRING]

            def release_block(b, name, key):
                noted["last use of block", b] = (name, key)

            def item_const():
                pe.wait_ge(*done("small_in_cst", ("cst", 1)))
                pe.wait_ge(*done("init"))

            def item_modcols(l):
                pe.wait_ge(*done("small_in_col", ("col", l, 7)))
                take([0], ("cols_copied", l))
                tr(pb[:, 0, 0:64], big[0:64, 1280:1408])
                for j in range(10):
                    last = tr(pb[:, 0, 64 + 6 * j:70 + 6 * j], big[0:6, j * P:j * P + P])
                last.then_inc(*tick("cols_full", l))
                for k in range(4):
                    take([1 + k % 2], ("keys_copied", (l, k)))
                    for i in range(4):
                        last = tr(pb[:, 1 + k % 2, i * P:i * P + P], big_at(1408, 16, P)[:, 4 * k + i, :])
                    last.then_inc(*tick("keys_full", (l, k)))
                pe.wait_ge(*done("c_silu"))
                if l:
                    take([3], ("mod_copied", (l, 1)))

            def item_modblocks(l, k0, k1):
                for k in range(k0, k1):
                    b, w = next_block()
                    for half in range(2):
                        j = 2 * k + half
                        for c in range(DC):
                            last = mm(modps(l)[:, 2 * j:2 * j + 2], w[:, c, half * P:half * P + P], cT[:, :, c],
                                      start=c == 0, stop=c == DC - 1)
                    last.then_inc(*tick("mod_full", (l, k)))
                    release_block(b, "mod_full", (l, k))

            def st_mod(u):
                item_modcols(1)
                item_modblocks(1, 0, 24)

            def transpose_rows(src, nk, banks, full, until, key):
                for k in range(nk):
                    take([banks[k]], (until, (key, k)))
                    for i in range(4):
                        last = tr(pb[:, banks[k], i * P:i * P + P], src[:, (4 * k + i) * P:(4 * k + i + 1) * P])
                    last.then_inc(*tick(full, (key, k)))

            def sum_squares(u, which):
                g, l, nt, NC, c0 = dims(u)
                pe.wait_ge(*done("squares", (u, which)))
                take([0], ("rms_read", (u, which)))
                for c in range(DC):
                    last = mm(pb[:, 0, 0:NC], ones, big_at(0, DC, NC)[:, c, :], start=c == 0, stop=c == DC - 1)
                last.then_inc(*tick("rms_full", (u, which)))

            def st_load(u):
                g, l, nt, NC, c0 = dims(u)
                if l == 0:
                    for i in range(nt):
                        pe.wait_ge(*done("small_in_x", ("x", u, nt - 1)))
                        transpose_rows(ycat[:, i, :], 2, [2 * i, 2 * i + 1], "x_full_", "x_copied_", (u, i))

            def st_norm1(u):
                sum_squares(u, 0)
                gap(u, "norm1", 0)

            def st_proj(u):
                g, l, nt, NC, c0 = dims(u)
                pe.wait_ge(*done("h_ready", (u, 0)))
                for jb in range(6):
                    b, w = next_block()
                    for half in range(2):
                        j = 2 * jb + half
                        take([j % 2], ("proj_copied", (u, j)))
                        for c in range(DC):
                            last = mm(pb[:, j % 2, 0:NC], w[:, c, half * P:half * P + P], hT[:, c, 0:NC],
                                      start=c == 0, stop=c == DC - 1)
                        last.then_inc(*tick("proj_full", (u, j)))
                        gap(u, "proj", j)
                    release_block(b, "proj_full", (u, j))
                n = 0
                for k in range(4):
                    b, w = next_block()
                    for i in range(nt):
                        bank = 2 + n % 4
                        n += 1
                        take([bank], ("tokcols_copied", (u, k, i)))
                        for c in range(DC):
                            last = mm(pb[:, bank, 0:WB], hT[:, c, i * P:i * P + P], w[:, c, :],
                                      start=c == 0, stop=c == DC - 1)
                        last.then_inc(*tick("tokcols_full", (u, k, i)))
                    release_block(b, "tokcols_full", (u, k, nt - 1))
                    gap(u, "proj", 12 + k)
                for i in range(2):
                    pe.wait_ge(*done("small_in_wsm", ("wsm", l, i)))
                for i in range(nt):
                    take([i], ("raw_copied", (u, i)))
                    for c in range(DC):
                        last = mm(pb[:, i, 0:24], hT[:, c, i * P:i * P + P], wsm[:, c, :], start=c == 0, stop=c == DC - 1)
                    last.then_inc(*tick("raw_full", (u, i)))
            def hpos(h):
                return (h % 2) * 2 + h // 2

            def st_scal(u):
                g, l, nt, NC, c0 = dims(u)
                gap(u, "scal", 0)
                pe.wait_ge(*done("lat_ready", u))
                take([2], ("sums_copied", u))
                for i in range(nt):
                    for d in range(2):
                        dst = pb[:, 2, i * 32:i * 32 + 16].rearrange("p (m d h) -> p m d h", m=2, d=2)[:, :, d, :]
                        src = lat[:, i, :].rearrange("p (m d h) -> p m d h", m=2, d=2)[:, :, d, :]
                        mm(dst, con("tri", d, P), src)
                    last = mm(pb[:, 2, i * 32 + 16:i * 32 + 32], ones, lat[:, i, :])
                last.then_inc(*tick("sums_full", u))

            def st_pre(u):
                g, l, nt, NC, c0 = dims(u)
                pe.wait_ge(*done("qk_squares", u))
                for j in range(4):
                    take([j], ("l2_read", u))
                    last = mm(pb[:, j, 0:NC], blk, big_at(0, 4, NC)[:, j, :])
                last.then_inc(*tick("l2_full", u))
                gap(u, "pre", 0)
                pe.wait_ge(*done("qk_normed", u))
                for i in range(nt):
                    for bank, js, full, until in ((4, (0, 1, 2), "xB_full", "xB_copied"), (5, (6, 7, 8, 9), "kv_full", "kv_copied")):
                        take([bank], (until, (u, i)))
                        for n, j in enumerate(js):
                            last = tr(pb[:, bank, n * P:n * P + P], cv[:, j, i * P:i * P + P])
                        last.then_inc(*tick(full, (u, i)))

            def st_intra(u, i):
                g, l, nt, NC, c0 = dims(u)
                t0 = slice(i * P, i * P + P)
                for d in range(2):
                    pe.wait_ge(*done("summands_ready", (u, i, d)))
                    take([2 * d, 2 * d + 1], ("rows_read", (u, i, d)))
                    for m in range(2):
                        last = mm(pb[:, 2 * d + m, :], ones, big[:, d * 1024 + m * 512:d * 1024 + m * 512 + 512])
                    last.then_inc(*tick("rows_full", (u, i, d)))
                take([4, 5], ("cb_read", (u, i)))
                for gr in range(2):
                    s = slice(64 * gr, 64 * gr + 64)
                    last = mm(pb[:, 4 + gr, 0:P], cv[s, 2, t0], cv[s, 3, t0])
                last.then_inc(*tick("cb_full", (u, i)))
                gap(u, f"intra{i}", 0)
                for base, qk in ((0, 6), (2, 4)):
                    take([base, base + 1], ("kk_read" if base == 0 else "qk_read", (u, i)))
                    for h in range(HEADS):
                        s = slice(64 * (h % 2), 64 * (h % 2) + 64)
                        last = mm(pb[:, base + h % 2, h // 2 * P:h // 2 * P + P], cv[s, 6 + h // 2, t0], cv[s, qk + h // 2, t0])
                    last.then_inc(*tick("kk_full" if base == 0 else "qk_full", (u, i)))
                gap(u, f"intra{i}", 1)
                for d in range(2):
                    pe.wait_ge(*done("beta_diag", (u, i, d)))
                    take([4 + d], ("n_ready", (u, i, d)))
                    mm(pb[:, 4 + d, :], ones, big_at(4096 + 512 * d, 512)).then_inc(*tick("beta_full", (u, i, d)))
                pe.wait_ge(*done("cb_read", (u, i)))
                take([0], ("y_read", (u, i)))
                for h in range(HEADS):
                    for d in range(2):
                        last = mm(pb[:, 0, h * HD:h * HD + HD], big_at(2048 + 512 * d, 4, P)[:, h, :],
                                  big_at(3072 + 256 * d, 4, HD)[:, h, :], start=d == 0, stop=d == 1)
                last.then_inc(*tick("y_full", (u, i)))
                gap(u, f"intra{i}", 2)
                for d in range(2):
                    pe.wait_ge(*done("xt_ready", (u, i, d, 0)))
                    take([2 + d], ("x0_ready", (u, i, d, 0)))
                    for n in range(4):
                        last = tr(pb[:, 2 + d, n * P:n * P + P], big_at(2048 + 512 * d, 4, P)[:, n, :])
                    last.then_inc(*tick("x_full", (u, i, d, 0)))
                for lv in range(1, LEVELS):
                    for d in range(2):
                        pe.wait_ge(*done("noff_ready", (u, i, d, lv)))
                        pe.wait_ge(*done("x_ready" if lv > 1 else "x0_ready", (u, i, d, lv - 1)))
                        take([d], ("p_copied", (u, i, d, lv)))
                        for n in range(4):
                            last = mm(pb[:, d, n * P:n * P + P], big_at(4096 + 512 * d, 4, P)[:, n, :],
                                      big_at(1024 + 512 * d, 4, P)[:, n, :])
                        last.then_inc(*tick("p_full", (u, i, d, lv)))
                    for d in range(2):
                        pe.wait_ge(*done("p_copied", (u, i, d, lv)))
                        if lv < LEVELS - 1:
                            take([2 + d], ("x_ready", (u, i, d, lv)))
                            for n in range(4):
                                last = mm(pb[:, 2 + d, n * P:n * P + P], big_at(2048 + 512 * d, 4, P)[:, n, :],
                                          big_at(3072 + 512 * d, 4, P)[:, n, :])
                            last.then_inc(*tick("x_full", (u, i, d, lv)))
                        take([4 + d], ("xt_ready", (u, i, d, lv)))
                        for n in range(4):
                            last = mm(pb[:, 4 + d, n * P:n * P + P], big_at(3072 + 512 * d, 4, P)[:, n, :],
                                      big_at(2048 + 512 * d, 4, P)[:, n, :])
                        last.then_inc(*tick("xt_full", (u, i, d, lv)))
                    gap(u, f"intra{i}", 2 + lv)
                pe.wait_ge(*done("xt_ready", (u, i, 1, LEVELS - 1)))
                pe.wait_ge(*done("rhs_ready", (u, i)))
                take([0], ("u_copied", (u, i)))
                for d in range(2):
                    for h in range(HEADS):
                        last = mm(pb[:, 0, d * 256 + h * HD:d * 256 + h * HD + HD],
                                  big_at(2048 + 512 * d, 4, P)[:, hpos(h), :], big_at(256 * d, 4, HD)[:, h, :])
                last.then_inc(*tick("u_full", (u, i)))
                if g:
                    take([1], ("wt_copied", (u, i)))
                    for d in range(2):
                        for h in range(HEADS):
                            s = slice(64 * (h % 2), 64 * (h % 2) + 64)
                            o = d * 256 + h // 2 * P
                            last = mm(pb[s, 1, o:o + P], big_at(512 + 256 * d, 4, HD)[:, h, :],
                                      big_at(2048 + 512 * d, 4, P)[:, hpos(h), :])
                    last.then_inc(*tick("wt_full", (u, i)))
                gap(u, f"intra{i}", 9)

            def st_scan(u):
                g, l, nt, NC, c0 = dims(u)
                pe.wait_ge(*done("u_copied", (u, nt - 1)))
                if g == 0:
                    take([0], ("ssd_out", u))
                    for d in range(2):
                        for gr in range(2):
                            last = mm(pb[:, 0, d * P + gr * 64:d * P + gr * 64 + 64], xe[:, d, gr * P:gr * P + P],
                                      tok[:, 0, 256 + gr * 64:320 + gr * 64])
                    last.then_inc(*tick("ssd_state_full", u))
                    take([1], ("gdn_out", u))
                    for d in range(2):
                        for pair in range(2):
                            o = (2 * d + pair) * P
                            last = mm(pb[:, 1, o:o + P], ke[:, d, pair * P:pair * P + P], sol[:, 0, d, pair * P:pair * P + P])
                    last.then_inc(*tick("gdn_state_full", u))
                else:
                    for d in range(2):
                        for k in range(2):
                            pe.wait_ge(*done("small_in_st", ("st", u, d, k)))
                            pe.wait_ge(*done("small_in_sgd", ("sgd", u, d, k)))
                    take([0], ("h_loaded", u))
                    for d in range(2):
                        last = tr(pb[:, 0, d * P:d * P + P], stn[:, d * P:d * P + P])
                    last.then_inc(*tick("h_loaded_full", u))
                    pe.wait_ge(*done("h_loaded", u))
                    pe.wait_ge(*done("wt_copied", (u, nt - 1)))
                    for turn in range(2):
                        for d in range(2):
                            i = d if turn == 0 else 1 - d
                            t0 = slice(i * P, i * P + P)
                            k = (u, turn, d)
                            if turn:
                                pe.wait_ge(*done("state_ready", (u, d)))
                            take([0, 1], ("yoff_read", k))
                            for gr in range(2):
                                s = slice(64 * gr, 64 * gr + 64)
                                last = mm(pb[:, gr, 0:P], cv[s, 3, t0], hst[s, d, :])
                            last.then_inc(*tick("yoff_full", k))
                            take([2, 3], ("v_ready", k))
                            for h in range(HEADS):
                                s = slice(64 * (h % 2), 64 * (h % 2) + 64)
                                o = d * 256 + h // 2 * P
                                last = mm(pb[:, 2 + h % 2, h // 2 * 64:h // 2 * 64 + 64], solW[s, i, o:o + P],
                                          sgd[s, d, h // 2, :])
                            last.then_inc(*tick("w_full", k))
                            take([4, 5], ("qs_read", k))
                            for h in range(HEADS):
                                s = slice(64 * (h % 2), 64 * (h % 2) + 64)
                                last = mm(pb[:, 4 + h % 2, h // 2 * 64:h // 2 * 64 + 64], cv[s, 4 + h // 2, t0],
                                          sgd[s, d, h // 2, :])
                            last.then_inc(*tick("qs_full", k))
                            gap(u, "scan", 2 * d if turn == 0 else 4 + d)
                            if turn == 0:
                                take([0], ("h_updated", (u, d)))
                                mm(pb[:, 0, 0:256], tok[:, i, 256:384], xe[:, d, :]).then_inc(*tick("dh_full", (u, d)))
                                pe.wait_ge(*done("v_ready", k))
                                take([2], ("state_ready", (u, d)))
                                for pair in range(2):
                                    last = mm(pb[:, 2, pair * P:pair * P + P], ke[:, d, pair * P:pair * P + P],
                                              sol[:, i, d, pair * P:pair * P + P])
                                last.then_inc(*tick("ds_full", (u, d)))
                                gap(u, "scan", 2 * d + 1)
                    pe.wait_ge(*done("v_ready", (u, 1, 1)))
                for i in range(nt):
                    take([2 + i], ("o_read", (u, i)))
                    for h in range(HEADS):
                        for d in range(2):
                            last = mm(pb[:, 2 + i, h * HD:h * HD + HD], attnT[:, i, d, hpos(h) * P:hpos(h) * P + P],
                                      sol[:, i, d, h * HD:h * HD + HD], start=d == 0, stop=d == 1)
                    last.then_inc(*tick("o_full", (u, i)))
                gap(u, "scan", 6)

            def st_fnet(u):
                g, l, nt, NC, c0 = dims(u)
                for i in range(nt):
                    for ct in range(2):
                        take([ct + 2 * i], ("xcs_copied", (u, i, ct)))
                        mm(pb[:, ct + 2 * i, 0:256], fnx[:, ct, i * P:i * P + P], con("chan")) \
                            .then_inc(*tick("xcs_full", (u, i, ct)))
                pe.wait_ge(*done("xcs_copied", (u, nt - 1, 1)))
                dft = con("dftS" if g else "dftP").rearrange("p (i s l) -> p i s l", i=nt, s=2)
                for t in range(nt):
                    take([4 + t], ("fnet_copied", (u, t)))
                    n = 0
                    for i in range(nt):
                        for s in range(2):
                            n += 1
                            last = mm(pb[:, 4 + t, 0:256], dft[:, i, s, t * P:t * P + P],
                                      big_at(i * 512, 2, 256)[:, :, s * P:s * P + P], start=n == 1, stop=n == 2 * nt)
                    last.then_inc(*tick("fnet_full", (u, t)))

            def st_attp(u):
                g, l, nt, NC, c0 = dims(u)
                gap(u, "attp", 0)
                for i in range(nt):
                    pe.wait_ge(*done("qk_rows", (u, i)))
                    take([i], ("qkT_copied", (u, i)))
                    for n in range(3):
                        last = tr(pb[:, i, n * P:n * P + P], big_at(i * 384, 384)[:, n * P:n * P + P])
                    last.then_inc(*tick("qkT_full", (u, i)))
                if g:
                    pe.wait_ge(*done("small_in_vc", ("vc", u, 0)))
                    pe.wait_ge(*done("small_in_vc", ("vc", u, 1)))
                    take([2], ("kcT_copied", u))
                    tr(pb[:, 2, 0:P], vc[:, 0, :]).then_inc(*tick("kcT_full", u))
                    pe.wait_ge(*done("kcT_copied", u))
                pe.wait_ge(*done("qkT_copied", (u, nt - 1)))

            def st_att(u, i):
                g, l, nt, NC, c0 = dims(u)
                nk = 3 if g else 1
                for h in range(HEADS):
                    s = slice(64 * (h // 2), 64 * (h // 2) + 64)
                    take([h], ("scores_read", (u, i)))
                    last = mm(pb[:, h, 0:nk * P], qTt[s, i, h % 2, :], kTt[s, 0:nk, :])
                last.then_inc(*tick("scores_full", (u, i)))
                gap(u, f"att{i}", 1)
                for h in range(HEADS):
                    pe.wait_ge(*done("probs_ready", (u, i, h)))
                    take([4 + h % 2], ("pT_copied", (u, i, h)))
                    for kb in range(nk):
                        last = tr(pb[:, 4 + h % 2, kb * P:kb * P + P], big_at(1024 + h * 384, 384)[:, kb * P:kb * P + P])
                    last.then_inc(*tick("pT_full", (u, i, h)))
                take([0], ("att_read", (u, i)))
                for h in range(HEADS):
                    pe.wait_ge(*done("pT_copied", (u, i, h)))
                    gr = h // 2
                    for kb in range(nk):
                        v = vc[:, 1, gr * 64:gr * 64 + 64] if kb == 2 else qkv[:, kb, 384 + gr * 64:448 + gr * 64]
                        last = mm(pb[:, 0, h * HD:h * HD + HD], big_at(2560 + h * 384, 384)[:, kb * P:kb * P + P], v,
                                  start=kb == 0, stop=kb == nk - 1)
                last.then_inc(*tick("att_full", (u, i)))
                gap(u, f"att{i}", 2)

            def st_out(u):
                g, l, nt, NC, c0 = dims(u)
                pe.wait_ge(*done("att_read", (u, nt - 1)))
                pe.wait_ge(*done("fnet_copied", (u, nt - 1)))
                for i in range(nt):
                    transpose_rows(ycat[:, i, :], 2, [2 * i, 2 * i + 1], "y_full_T", "yT_copied", (u, i))
                for i in range(nt):
                    pe.wait_ge(*done("yT_copied", ((u, i), 1)))
                for k in range(4):
                    b, w = next_block()
                    for half in range(2):
                        j = 2 * k + half
                        take([4 + j % 2], ("x_added", (u, j)))
                        for c in range(DC):
                            last = mm(pb[:, 4 + j % 2, 0:NC], w[:, c, half * P:half * P + P], hT[:, c, 0:NC],
                                      start=c == 0, stop=c == DC - 1)
                        last.then_inc(*tick("out_full", (u, j)))
                        gap(u, "out", j)
                    release_block(b, "out_full", (u, j))

            def st_query(u):
                g, l, nt, NC, c0 = dims(u)
                sum_squares(u, 1)
                gap(u, "query", 0)
                pe.wait_ge(*done("h_ready", (u, 1)))
                for i in range(nt):
                    for k in range(2):
                        take([2 * i + k], ("h2_copied", (u, i, k)))
                        for c in range(4):
                            last = tr(pb[:, 2 * i + k, c * P:c * P + P], hT[:, 4 * k + c, i * P:i * P + P])
                        last.then_inc(*tick("h2_full", (u, i, k)))
                for k in range(8):
                    b, w = next_block()
                    for half in range(2):
                        j = 2 * k + half
                        take([4 + j % 2], ("q_copied", (u, j)))
                        for c in range(DC):
                            last = mm(pb[:, 4 + j % 2, 0:NC], w[:, c, half * P:half * P + P], hT[:, c, 0:NC],
                                      start=c == 0, stop=c == DC - 1)
                        last.then_inc(*tick("q_full", (u, j)))
                        gap(u, "query", 1 + j)
                    release_block(b, "q_full", (u, j))
                pe.wait_ge(*done("q_copied", (u, 15)))
                for i in range(nt):
                    for k in range(4):
                        take([k], ("s_copied", (u, i, k)))
                        for n in range(4):
                            last = mm(pb[:, k, n * P:n * P + P], big_at(0, 16, NC)[:, 4 * k + n, i * P:i * P + P],
                                      keysT[:, 4 * k + n, :])
                        last.then_inc(*tick("s_full", (u, i, k)))

            def item_v(q, t, i0, i1, halves, slots):
                nv = v_before["v", q]
                if i0 == 0 and 0 in halves:
                    if nv:
                        pe.wait_ge(*done("v_summed", q - 1))
                    else:
                        pe.wait_ge(*done("mod_copied", (0, 1)))
                        for h in range(2):
                            mm(pv[:, 0, 0:2], zero[:, :], zero[:, 0:2]).then_inc(used_pe[h], 1)
                    for k in range(2):
                        mm(pv[:, k, :], zero[:, :], cst[:, 0:512], start=True, stop=False)
                ph = phase_of["v", q]
                with steps(pe, i0, i1) as i:
                    for h in halves:
                        pe.wait_ge(diag_ready[h], i + (nv * STEPS + 1))
                        for n in range(slots):
                            j = h * HB + n
                            pe.wait_ge(rows_in[j], i * 16 + 16 * (ph * STEPS + 1))
                            for k in range(2):
                                last = mm(pv[:, k, :], diag[:, h * PE_SLOTS + n, :], ring[:, j, k * 512:k * 512 + 512], start=False, stop=False)
                        last.then_inc(used_pe[h], 1)
                if i1 == STEPS and 1 in halves:
                    mm(pv[:, 0, :], zero[:, :], cst[:, 0:512], start=False, stop=True)
                    mm(pv[:, 1, :], zero[:, :], cst[:, 0:512], start=False, stop=True).then_inc(*tick("v_full", q))

            def item_end(u, q, t):
                pe.wait_ge(*done("v_summed", q))
                for k in range(2):
                    take([k], ("x_added2", (q, k)))
                    for c in range(4):
                        last = tr(pb[:, k, c * P:c * P + P], accv[:, (4 * k + c) * P:(4 * k + c + 1) * P])
                    last.then_inc(*tick("acc_full", (q, k)))

            def item_final():
                pe.wait_ge(*done("x_added2", (5, 1)))
                for t in range(3):
                    for k in range(2):
                        n = 2 * t + k
                        take([n], ("x_out_copied", (t, k)))
                        for c in range(4):
                            last = tr(pb[:, n, c * P:c * P + P], xT[:, 4 * k + c, t * P:t * P + P])
                        last.then_inc(*tick("x_out_full", (t, k)))

            stages = {"load": st_load, "norm1": st_norm1, "proj": st_proj, "scal": st_scal, "pre": st_pre,
                      "intra0": lambda u: st_intra(u, 0), "intra1": lambda u: st_intra(u, 1), "scan": st_scan,
                      "fnet": st_fnet, "attp": st_attp, "att0": lambda u: st_att(u, 0), "att1": lambda u: st_att(u, 1),
                      "out": st_out, "query": st_query, "mod": st_mod}
            gap, run = engine_schedule({"const": item_const, "modcols": item_modcols, "modblocks": item_modblocks,
                                        "v": item_v, "end": item_end, "final": item_final}, stages)
            run()

        @block.scalar
        def _(act):
            step, stepped = stepper("act_step")

            def fn(out, in_, f=ACT.Copy, **kw):
                return nc.scalar.activation(out, in_, f, **kw)

            def item_const():
                act.wait_ge(*done("small_in_cst", ("cst", 1)))
                act.wait_ge(*done("small_in_cT", ("cT", 0)))
                act.wait_ge(*done("small_in_cT", ("cT", 1)))
                act.wait_ge(*done("init"))
                fn(cT[:, :, :], cT[:, :, :], ACT.Silu).then_inc(*tick("c_silu"))

            def item_modcols(l):
                act.wait_ge(*done("cols_full", l))
                fn(colT[:, :], pb[:, 0, 0:64]).then_inc(*step())
                act.wait_ge(*stepped())
                fn(convT[:, :, :], pb[:, 0, 64:124].rearrange("p (a b) -> p a b", b=6)).then_inc(*tick("cols_copied", l))
                for k in range(4):
                    act.wait_ge(*done("keys_full", (l, k)))
                    fn(keysT[:, 4 * k:4 * k + 4, :], pb[:, 1 + k % 2, :].rearrange("p (a b) -> p a b", b=P)) \
                        .then_inc(*tick("keys_copied", (l, k)))

            def norm(u, which):
                g, l, nt, NC, c0 = dims(u)
                if which == 0 and l == 0:
                    for i in range(nt):
                        act.wait_ge(*done("x_copied_", ((u, i), 1)))
                elif which == 0:
                    for q, t in seq_tiles(u - 2):
                        act.wait_ge(*done("x_added2", (q, 1)))
                else:
                    act.wait_ge(*done("x_added", (u, 7)))
                if u:
                    act.wait_ge(*done("mix_done", u - 1))
                if which and g == 0:
                    for name in ("out_k", "out_v", "out_ssd", "out_gdn"):
                        act.wait_ge(sem(name), counts[name])
                fn(big_at(0, DC, NC), xT[:, :, c0:c0 + NC], ACT.Square).then_inc(*tick("squares", (u, which)))
                act.wait_ge(*done("rms_full", (u, which)))
                fn(big_at(2048, NC), pb[:, 0, 0:NC], ACT.Sqrt, scale=1.0 / D, bias=epsc[:, 0:1]) \
                    .then_inc(*tick("rms_read", (u, which)))
                gap(u, "query" if which else "norm1", 0)
                act.wait_ge(*done("h_normed", (u, which)))
                act.wait_ge(*done("modA_ready", (l, which)))
                sh = 24 * which
                for c in range(DC):
                    last = fn(hT[:, c, 0:NC], hT[:, c, 0:NC], ACT.Identity, scale=modA[:, l, which, c, g:g + 1],
                              bias=modT[:, l, sh + c, g:g + 1])
                last.then_inc(*tick("h_ready", (u, which)))

            def st_load(u):
                g, l, nt, NC, c0 = dims(u)
                if l == 0:
                    for i in range(nt):
                        for k in range(2):
                            act.wait_ge(*done("x_full_", ((u, i), k)))
                            fn(xT[:, 4 * k:4 * k + 4, c0 + i * P:c0 + i * P + P],
                                    pb[:, 2 * i + k, :].rearrange("p (a b) -> p a b", b=P)) \
                                        .then_inc(*tick("x_copied_", ((u, i), k)))

            def st_proj(u):
                g, l, nt, NC, c0 = dims(u)
                cin = cinS if g else cinP
                act.wait_ge(*done("init"))

                def silu(j):
                    act.wait_ge(*done("conv_done", (u, j)))
                    fn(cv[:, j, 0:NC], big_at(2560 + 256 * (j % 2), NC), ACT.Silu, bias=convT[:, j, 5:6]) \
                        .then_inc(*tick("silu_done", (u, j)))

                for j in range(10):
                    act.wait_ge(*done("proj_full", (u, j)))
                    if j >= 2:
                        act.wait_ge(*done("conv_done", (u, j - 2)))
                    fn(cin[:, j % 2, 2:2 + NC], pb[:, j % 2, 0:NC]).then_inc(*tick("proj_copied", (u, j)))
                    if j:
                        silu(j - 1)
                    gap(u, "proj", j)
                silu(9)
                for j in range(2):
                    act.wait_ge(*done("proj_full", (u, 10 + j)))
                    fn(fnx[:, j, 0:NC], pb[:, j, 0:NC]).then_inc(*tick("proj_copied", (u, 10 + j)))
                    gap(u, "proj", 10 + j)
                n = 0
                for k in range(4):
                    for i in range(nt):
                        act.wait_ge(*done("tokcols_full", (u, k, i)))
                        src = pb[:, 2 + n % 4, 0:WB]
                        n += 1
                        last = (fn(zs[:, i, k, :], src, ACT.Silu) if k < 2 else
                                fn(qkv[:, i, (k - 2) * WB:(k - 2) * WB + WB], src))
                        last.then_inc(*tick("tokcols_copied", (u, k, i)))
                    gap(u, "proj", 12 + k)
                for i in range(nt):
                    act.wait_ge(*done("raw_full", (u, i)))
                    fn(raw[:, i, :], pb[:, i, 0:24]).then_inc(*tick("raw_copied", (u, i)))

            def st_scal(u):
                g, l, nt, NC, c0 = dims(u)
                act.wait_ge(*done("small_in_prm", ("prm", l, 232)))
                fn(sca[:, 8, 0, 0:16], pr("A"), ACT.Exp)
                act.wait_ge(*done("neg_abs", u))
                fn(sca[:, 2, 0:nt, :], sca[:, 1, 0:nt, :], ACT.Exp).then_inc(*tick("exp_neg", u))
                gap(u, "scal", 0)
                act.wait_ge(*done("sums_full", u))
                fn(gct[:, 0:nt, :], pb[:, 2, 0:32 * nt].rearrange("p (a b) -> p a b", b=32)) \
                    .then_inc(*tick("sums_copied", u))
                act.wait_ge(*done("sums_copied", u))
                fn(ege[:, 0:nt, :], gct[:, 0:nt, :], ACT.Exp)
                gap(u, "scal", 1)
                act.wait_ge(*done("to_end", u))
                fn(dte[:, 0:nt, :], sca[:, 9, 0:nt, 0:16], ACT.Exp).then_inc(*tick("decays", u))

            def st_pre(u):
                g, l, nt, NC, c0 = dims(u)
                act.wait_ge(*done("silu_done", (u, 9)))
                fn(big_at(0, 4, NC), cv[:, 4:8, 0:NC], ACT.Square).then_inc(*tick("qk_squares", u))
                act.wait_ge(*done("l2_full", u))
                fn(big_at(2048, 4, NC), pb[:, 0:4, 0:NC], ACT.Sqrt, bias=epsc[:, 0:1]).then_inc(*tick("l2_read", u))
                gap(u, "pre", 0)
                for i in range(nt):
                    act.wait_ge(*done("xB_full", (u, i)))
                    fn(tok[:, i, 0:384], pb[:, 4, 0:384]).then_inc(*tick("xB_copied", (u, i)))
                    act.wait_ge(*done("kv_full", (u, i)))
                    fn(tok[:, i, 384:896], pb[:, 5, :]).then_inc(*tick("kv_copied", (u, i)))

            def st_intra(u, i):
                g, l, nt, NC, c0 = dims(u)
                gap(u, f"intra{i}", 0)
                for d in range(2):
                    act.wait_ge(*done("rows_read", (u, i, d)))
                    fn(dec[:, d, :, :], dec[:, d, :, :], ACT.Exp).then_inc(*tick("dec_ready", (u, i, d)))
                gap(u, f"intra{i}", 2)
                for d in range(2):
                    act.wait_ge(*done("x_full", (u, i, d, 0)))
                    fn(big_at(1024 + 512 * d, 512), pb[:, 2 + d, :]).then_inc(*tick("x0_ready", (u, i, d, 0)))
                for lv in range(1, LEVELS):
                    for d in range(2):
                        act.wait_ge(*done("p_full", (u, i, d, lv)))
                        fn(big_at(3072 + 512 * d, 512), pb[:, d, :]).then_inc(*tick("p_copied", (u, i, d, lv)))
                    gap(u, f"intra{i}", 2 + lv)
                act.wait_ge(*done("u_full", (u, i)))
                fn(sol[:, i, :, :], pb[:, 0, :].rearrange("p (a b) -> p a b", b=256)).then_inc(*tick("u_copied", (u, i)))
                if g:
                    act.wait_ge(*done("wt_full", (u, i)))
                    fn(solW[:, i, :], pb[:, 1, :]).then_inc(*tick("wt_copied", (u, i)))

            def st_scan(u):
                g, l, nt, NC, c0 = dims(u)
                if g == 0:
                    if u:
                        act.wait_ge(*done("mix_done", u - 1))
                    act.wait_ge(*done("ssd_state_full", u))
                    fn(stn[:, :], pb[:, 0, 0:256]).then_inc(*tick("ssd_out", u))
                    act.wait_ge(*done("ssd_out", u))
                    for d in range(2):
                        for r in range(4):
                            gr, rr = r // 2, r % 2
                            act.dma_start(outs["ssd"][0, l, d, r], stn[64 * rr:64 * rr + 64, d * P + gr * 64:d * P + gr * 64 + 64]) \
                                .then_inc(*tick("out_ssd", (u, d, r), 16))
                    act.wait_ge(*done("gdn_state_full", u))
                    for par in range(2):
                        s = slice(64 * par, 64 * par + 64)
                        last = fn(sgd[s, :, :, :].rearrange("p d a v -> p (d a) v"),
                                  pb[s, 1, :].rearrange("p (b v) -> p b v", b=4)[:, :, par * 64:par * 64 + 64])
                    last.then_inc(*tick("gdn_out", u))
                    act.wait_ge(*done("gdn_out", u))
                    for d in range(2):
                        for h in range(4):
                            par, pair = h % 2, h // 2
                            act.dma_start(outs["gdn"][0, l, d, h], sgd[64 * par:64 * par + 64, d, pair, :]) \
                                .then_inc(*tick("out_gdn", (u, d, h), 16))
                else:
                    act.wait_ge(*done("h_loaded_full", u))
                    fn(hst[:, :, :], pb[:, 0, 0:256].rearrange("p (a b) -> p a b", b=P)).then_inc(*tick("h_loaded", u))
                gap(u, "scan", 6)
                act.wait_ge(*done("ms_ready", u))
                fn(sm[:, 0:nt, :], sm[:, 2:2 + nt, :], ACT.Sqrt, scale=1.0 / HD, bias=epsc[:, 0:1]) \
                    .then_inc(*tick("ms_roots", u))

            def st_fnet(u):
                g, l, nt, NC, c0 = dims(u)
                act.wait_ge(*done("rhs_ready", (u, nt - 1)))
                for i in range(nt):
                    for ct in range(2):
                        act.wait_ge(*done("xcs_full", (u, i, ct)))
                        fn(big_at(i * 512 + ct * 256, 256), pb[:, ct + 2 * i, 0:256]) \
                            .then_inc(*tick("xcs_copied", (u, i, ct)))
                for t in range(nt):
                    act.wait_ge(*done("fnet_full", (u, t)))
                    fn(ycat[:, t, 512:768], pb[:, 4 + t, 0:256]).then_inc(*tick("fnet_copied", (u, t)))

            def st_attp(u):
                g, l, nt, NC, c0 = dims(u)
                act.wait_ge(*done("att_ms", u))
                fn(sm[:, 0:nt, 0:6], sm[:, 2:2 + nt, 0:6], ACT.Sqrt, scale=1.0 / HD, bias=epsc[:, 0:1]) \
                    .then_inc(*tick("att_roots", u))
                gap(u, "attp", 0)
                if g == 0:
                    act.wait_ge(*done("qk_rows", (u, 0)))
                    act.dma_start(outs["k"][0, l].rearrange("s h d -> s (h d)"), big[:, 256:384]) \
                        .then_inc(*tick("out_k", u, 16))
                    act.dma_start(outs["v"][0, l].rearrange("s h d -> s (h d)"), qkv[:, 0, 384:512]) \
                        .then_inc(*tick("out_v", u, 16))
                for i in range(nt):
                    act.wait_ge(*done("qkT_full", (u, i)))
                    fn(qTt[:, i, :, :], pb[:, i, 0:256].rearrange("p (a b) -> p a b", b=P)).then_inc(*step())
                    act.wait_ge(*stepped())
                    fn(kTt[:, i, :], pb[:, i, 256:384]).then_inc(*tick("qkT_copied", (u, i)))
                if g:
                    act.wait_ge(*done("kcT_full", u))
                    fn(kTt[:, 2, :], pb[:, 2, 0:P]).then_inc(*tick("kcT_copied", u))

            def st_att(u, i):
                g, l, nt, NC, c0 = dims(u)
                nk = 3 if g else 1
                gap(u, f"att{i}", 0)
                act.wait_ge(*done("max_ready", (u, i)))
                for h in range(HEADS):
                    pr_h = big_at(1024 + h * 384, nk * P)
                    fn(pr_h, pr_h, ACT.Exp, scale=HD ** -0.5, bias=sm[:, 4, h:h + 1], accum_out=sm[:, 5, h:h + 1]) \
                        .then_inc(*tick("probs_ready", (u, i, h)))
                fn(sm[:, 6, 0:4], sm[:, 6, 4:8], ACT.Exp).then_inc(*tick("sink_ready", (u, i)))
                gap(u, f"att{i}", 1)
                for h in range(HEADS):
                    act.wait_ge(*done("pT_full", (u, i, h)))
                    fn(big_at(2560 + h * 384, nk * P), pb[:, 4 + h % 2, 0:nk * P]).then_inc(*tick("pT_copied", (u, i, h)))

            def st_out(u):
                g, l, nt, NC, c0 = dims(u)
                for i in range(nt):
                    for k in range(2):
                        act.wait_ge(*done("y_full_T", ((u, i), k)))
                        fn(hT[:, 4 * k:4 * k + 4, i * P:i * P + P], pb[:, 2 * i + k, :].rearrange("p (a b) -> p a b", b=P)) \
                            .then_inc(*tick("yT_copied", ((u, i), k)))

            def st_query(u):
                g, l, nt, NC, c0 = dims(u)
                norm(u, 1)
                for i in range(nt):
                    t = GROUP_TILES[g][i]
                    for k in range(2):
                        act.wait_ge(*done("h2_full", (u, i, k)))
                        fn(h2[:, t, 512 * k:512 * k + 512], pb[:, 2 * i + k, :]).then_inc(*tick("h2_copied", (u, i, k)))
                for j in range(16):
                    act.wait_ge(*done("q_full", (u, j)))
                    fn(big_at(0, 16, NC)[:, j, :], pb[:, 4 + j % 2, 0:NC]).then_inc(*tick("q_copied", (u, j)))
                    gap(u, "query", 1 + j)
                for i in range(nt):
                    for k in range(4):
                        act.wait_ge(*done("s_full", (u, i, k)))
                        dst = cv[:, 0:8, :].rearrange("p a b -> p (a b)") if i else dec[:, :, :, :].rearrange("p a b c -> p (a b c)")
                        fn(dst[:, 512 * k:512 * k + 512], pb[:, k, :]).then_inc(*tick("s_copied", (u, i, k)))

            def st_topk(u, i):
                gap(u, f"topk{i}", 8)
                act.wait_ge(*done("best_shifted", (u, i)))
                t = GROUP_TILES[UNITS[u][0]][i]
                fn(gatew[:, t, :], gatew[:, t, :], ACT.Exp).then_inc(*tick("gate_exp", (u, i)))

            def item_gelu(q, t):
                act.wait_ge(dots_kept, (phase_of["u", q] - v_before["u", q] + 1) * STEPS * 2)
                fn(dots[:, t, :], dots[:, t, :], ACT.Gelu).then_inc(*tick("gelu_done", q))

            def item_v(q, t, i0, i1, halves, slots):
                nv, ph = v_before["v", q], phase_of["v", q]
                if i0 == 0 and 0 in halves:
                    act.wait_ge(*done("w_ready", q))
                with steps(act, i0, i1) as i:
                    for h in halves:
                        act.wait_ge(used_pe[h], i + (nv * STEPS + 1))
                        for n in range(slots):
                            j = h * HB + n
                            last = fn(diag[:, h * PE_SLOTS + n, :], ident, ACT.Copy, scale=dots[:, t, bass.ds(i * STEP + j, 1)])
                        last.then_inc(diag_ready[h], 1)

            def item_final():
                for t in range(3):
                    for k in range(2):
                        act.wait_ge(*done("x_out_full", (t, k)))
                        fn(h2[:, t, 512 * k:512 * k + 512], pb[:, 2 * t + k, :]).then_inc(*tick("x_out_copied", (t, k)))
                    act.wait_ge(*done("x_out_copied", (t, 1)))
                    dst = outs["yp"][0] if t == 0 else outs["ys"][0, (t - 1) * P:t * P, :]
                    act.dma_start(dst, h2[:, t, :]).then_inc(*tick("out_y", t, 16))
                for name in ("out_y", "out_ssd", "out_gdn", "out_k", "out_v"):
                    act.wait_ge(sem(name), counts[name])

            stages = {"load": st_load, "norm1": lambda u: norm(u, 0), "proj": st_proj, "scal": st_scal, "pre": st_pre,
                      "intra0": lambda u: st_intra(u, 0), "intra1": lambda u: st_intra(u, 1), "scan": st_scan,
                      "fnet": st_fnet, "attp": st_attp, "att0": lambda u: st_att(u, 0), "att1": lambda u: st_att(u, 1),
                      "out": st_out, "query": st_query, "topk0": lambda u: st_topk(u, 0), "topk1": lambda u: st_topk(u, 1),
                      "mod": lambda u: item_modcols(1)}
            gap, run = engine_schedule({"const": item_const, "modcols": item_modcols, "gelu": item_gelu, "v": item_v,
                                        "final": item_final}, stages)
            run()

        @block.vector
        def _(dve):
            step, stepped = stepper("dve_step")
            added = [0]
            tt, ts, stt = dve.tensor_tensor, dve.tensor_scalar, dve.scalar_tensor_tensor

            def item_const():
                dve.wait_ge(*done("small_in_cst", ("cst", 1)))
                dve.tensor_copy(lvl[:, :, :, :].rearrange("p a b c -> p (a b c)"),
                                dec[:, :, :, :].rearrange("p a b c -> p (a b c)")[:, 0:2 * LEVELS * P])
                dve.memset(cinP[:, :, :], 0.0)
                dve.memset(cinS[:, :, :], 0.0)
                dve.memset(zero[:, :], 0.0)
                dve.memset(epsc[:, :], EPS).then_inc(*tick("init"))
                for h in range(2):
                    dve.memset(dot8[:, h * HB:h * HB + 1], 0.0).then_inc(used_dve[h], 1)

            def item_modsum(l, which):
                dve.wait_ge(*done("cols_copied", l))
                dve.wait_ge(*done("mod_full", (l, 23 if which or l else 7)))
                j0, j1 = (16, 48) if which else (0, 16)
                tt(modT[:, l, j0:j1, :], modps(l)[:, 2 * j0:2 * j1].rearrange("p (a b) -> p a b", b=2),
                   bc2(colT[:, j0:j1], 2), ALU.add).then_inc(*tick("mod_copied", (l, which)))
                dve.wait_ge(*done("mod_copied", (l, which)))
                stt(modA[:, l, which, :, :], modT[:, l, 8 + 24 * which:16 + 24 * which, :], 1.0,
                    bc2(colT[:, 48 + 8 * which:56 + 8 * which], 2), ALU.add, ALU.mult).then_inc(*tick("modA_ready", (l, which)))

            def st_mod(u):
                gap(u, "mod", 23)
                for which in range(2):
                    item_modsum(1, which)

            def norm(u, which):
                g, l, nt, NC, c0 = dims(u)
                gap(u, "query" if which else "norm1", 0)
                dve.wait_ge(*done("rms_read", (u, which)))
                r = big_at(2048, NC)
                dve.reciprocal(r, r).then_inc(*step())
                dve.wait_ge(*stepped())
                tt(hT[:, :, 0:NC], xT[:, :, c0:c0 + NC], bc1(r, DC), ALU.mult).then_inc(*tick("h_normed", (u, which)))

            def st_proj(u):
                g, l, nt, NC, c0 = dims(u)
                cin = cinS if g else cinP
                dve.wait_ge(*done("cols_copied", l))
                for j in range(10):
                    gap(u, "proj", j)
                    dve.wait_ge(*done("proj_copied", (u, j)))
                    if j >= 2:
                        dve.wait_ge(*done("silu_done", (u, j - 2)))
                    y = big_at(2560 + 256 * (j % 2), NC)
                    ts(y, cin[:, j % 2, 0:NC], convT[:, j, 0:1], None, ALU.mult).then_inc(*step())
                    dve.wait_ge(*stepped())
                    for k in range(1, CONV_W):
                        last = stt(y, cin[:, j % 2, k:k + NC], convT[:, j, k:k + 1], y, ALU.mult, ALU.add)
                        if k < CONV_W - 1:
                            last.then_inc(*step())
                            dve.wait_ge(*stepped())
                    last.then_inc(*tick("conv_done", (u, j)))

            def st_scal(u):
                g, l, nt, NC, c0 = dims(u)
                for i in range(nt):
                    dve.wait_ge(*done("raw_copied", (u, i)))
                dve.wait_ge(*done("small_in_prm", ("prm", l, 232)))
                s = lambda k, n=16: sca[:, k, 0:nt, 0:n]
                tt(s(0), raw[:, 0:nt, 0:16], bc1(pr("bias"), nt), ALU.add).then_inc(*step())
                dve.wait_ge(*stepped())
                stt(s(1), s(0), -1.0, s(0), ALU.mult, ALU.min).then_inc(*step())
                dve.wait_ge(*stepped())
                ts(sca[:, 1, 0:nt, 16:24], raw[:, 0:nt, 16:24], -1.0, None, ALU.mult).then_inc(*tick("neg_abs", u))
                gap(u, "scal", 0)
                dve.wait_ge(*done("exp_neg", u))
                ts(s(3), s(2), 2.0, None, ALU.add).then_inc(*step())
                dve.wait_ge(*stepped())
                dve.reciprocal(s(3), s(3)).then_inc(*step())
                dve.wait_ge(*stepped())
                tt(s(4), s(2), s(3), ALU.mult).then_inc(*step())
                dve.wait_ge(*stepped())
                tt(s(5), s(4), s(4), ALU.mult).then_inc(*step())
                dve.wait_ge(*stepped())
                ts(s(6), s(5), 1.0 / 15, None, ALU.mult).then_inc(*step())
                dve.wait_ge(*stepped())
                for k in (13, 11, 9, 7, 5, 3):
                    stt(s(6), s(6), 1.0 / k, s(5), ALU.add, ALU.mult).then_inc(*step())
                    dve.wait_ge(*stepped())
                stt(s(6), s(6), 1.0, s(4), ALU.add, ALU.mult).then_inc(*step())
                dve.wait_ge(*stepped())
                ts(s(7), s(0), 0.0, None, ALU.max).then_inc(*step())
                dve.wait_ge(*stepped())
                stt(spt[:, 0:nt, :], s(6), 2.0, s(7), ALU.mult, ALU.add).then_inc(*step())
                dve.wait_ge(*stepped())
                stt(lat[:, 0:nt, :], spt[:, 0:nt, :], -1.0, bc1(sca[:, 8, 0, 0:16], nt), ALU.mult, ALU.mult) \
                    .then_inc(*tick("lat_ready", u))
                ts(sca[:, 3, 0:nt, 16:24], sca[:, 2, 0:nt, 16:24], 1.0, None, ALU.add).then_inc(*step())
                dve.wait_ge(*stepped())
                dve.reciprocal(bet[:, 0:nt, :], sca[:, 3, 0:nt, 16:24]).then_inc(*step())
                dve.wait_ge(*stepped())
                gap(u, "scal", 1)
                dve.wait_ge(*done("sums_copied", u))
                tt(s(9), gct[:, 0:nt, 16:32], gct[:, 0:nt, 0:16], ALU.subtract).then_inc(*tick("to_end", u))

            def st_pre(u):
                g, l, nt, NC, c0 = dims(u)
                gap(u, "pre", 0)
                dve.wait_ge(*done("l2_read", u))
                r = big_at(2048, 4, NC)
                dve.reciprocal(r, r).then_inc(*step())
                dve.wait_ge(*stepped())
                stt(cv[:, 4:6, 0:NC], cv[:, 4:6, 0:NC], HD ** -0.5, r[:, 0:2, :], ALU.mult, ALU.mult)
                tt(cv[:, 6:8, 0:NC], cv[:, 6:8, 0:NC], r[:, 2:4, :], ALU.mult).then_inc(*tick("qk_normed", u))

            def st_intra(u, i):
                g, l, nt, NC, c0 = dims(u)
                four = "p (m d h) -> p m d h"
                dve.wait_ge(*done("decays", u))
                dve.wait_ge(*done("kv_copied", (u, i)))
                for d in range(2):
                    la = lat[:, i, :].rearrange(four, m=2, d=2)[:, :, d, :]
                    dst = big_at(d * 1024, 1024).rearrange("p (m h j) -> p m h j", m=2, h=4)
                    tt(dst, bc1(bc1(con("tri", d, P), 4), 2), bc2(la, P), ALU.mult) \
                        .then_inc(*tick("summands_ready", (u, i, d)))
                for d in range(2):
                    b = bet[:, i, d * 4:d * 4 + 4].rearrange("p (pair par) -> p par pair", par=2)
                    tt(big_at(4096 + 512 * d, 2, 2, P), bc1(bc1(ident, 2), 2), bc2(b, P), ALU.mult) \
                        .then_inc(*tick("beta_diag", (u, i, d)))
                x4 = tok[:, i, 0:256].rearrange("p (h e) -> p h e", h=4)
                for d in range(2):
                    xdt = big_at(3072 + 256 * d, 4, HD)
                    tt(xdt, x4, bc2(spt[:, i, d * 4:d * 4 + 4], HD), ALU.mult).then_inc(*step())
                    dve.wait_ge(*stepped())
                    if g == 0 or d == i:
                        tt(xe[:, d, :].rearrange("p (h e) -> p h e", h=4), xdt, bc2(dte[:, i, d * 4:d * 4 + 4], HD), ALU.mult)
                        k4 = tok[:, i, 384:640].rearrange("p (h e) -> p h e", h=4)
                        tt(ke[:, d, :].rearrange("p (h e) -> p h e", h=4), k4, bc2(dte[:, i, 8 + d * 4:12 + d * 4], HD), ALU.mult)
                gap(u, f"intra{i}", 0)
                for d in range(2):
                    dve.wait_ge(*done("rows_full", (u, i, d)))
                    for m in range(2):
                        for h in range(4):
                            c = m * 8 + d * 4 + h
                            last = stt(dec[:, d, m * 4 + h, :], pb[:, 2 * d + m, h * P:h * P + P], gct[:, i, c:c + 1],
                                       con("negm", d, P), ALU.subtract, ALU.add)
                    last.then_inc(*tick("rows_read", (u, i, d)))
                gap(u, f"intra{i}", 1)
                dve.wait_ge(*done("cb_full", (u, i)))
                for d in range(2):
                    dve.wait_ge(*done("dec_ready", (u, i, d)))
                    cb = pb[:, 4:6, 0:P]
                    for r in range(2):
                        dst = big_at(2048 + 512 * d, 2, 2, P)[:, :, r, :]
                        src = dec[:, d, 0:4, :].rearrange("p (g r) j -> p g r j", g=2)[:, :, r, :]
                        last = tt(dst, cb, src, ALU.mult)
                last.then_inc(*tick("cb_read", (u, i)))
                dve.wait_ge(*done("qk_full", (u, i)))
                for d in range(2):
                    last = tt(attnT[:, i, d, :].rearrange("p (a b j) -> p a b j", a=2, b=2),
                              pb[:, 2:4, 0:256].rearrange("p a (b j) -> p a b j", b=2), heads_by_parity(dec[:, d, 4:8, :]), ALU.mult)
                last.then_inc(*tick("qk_read", (u, i)))
                dve.wait_ge(*done("kk_full", (u, i)))
                dve.wait_ge(*done("rows_full", (u, i, 1)))
                for d in range(2):
                    last = tt(big_at(512 * d, 2, 2, P), pb[:, 0:2, 0:256].rearrange("p a (b j) -> p a b j", b=2),
                              heads_by_parity(dec[:, d, 4:8, :]), ALU.mult)
                last.then_inc(*tick("kk_read", (u, i)))
                dve.wait_ge(*done("kk_read", (u, i)))
                gap(u, f"intra{i}", 2)
                for d in range(2):
                    dve.wait_ge(*done("beta_full", (u, i, d)))
                    stt(big_at(512 * d, 512), pb[:, 4 + d, :], -1.0, big_at(512 * d, 512), ALU.mult, ALU.mult) \
                        .then_inc(*tick("n_ready", (u, i, d)))
                dve.wait_ge(*done("n_ready", (u, i, 1)))
                dve.wait_ge(*done("y_full", (u, i)))
                y4 = ydg[:, i, :].rearrange("p (h e) -> p h e", h=4)
                tt(y4, x4, bc2(pr("D"), HD), ALU.mult).then_inc(*step())
                dve.wait_ge(*stepped())
                tt(ydg[:, i, :], ydg[:, i, :], pb[:, 0, 0:256], ALU.add).then_inc(*tick("y_read", (u, i)))

                def off(d, lv, dst):
                    return tt(dst, big_at(512 * d, 4, P), bc1(lvl[:, d, lv, :], 4), ALU.mult)

                for d in range(2):
                    xt = big_at(2048 + 512 * d, 4, P)
                    off(d, 0, xt).then_inc(*step())
                    dve.wait_ge(*stepped())
                    tt(xt, xt, bc1(ident, 4), ALU.add).then_inc(*tick("xt_ready", (u, i, d, 0)))
                for lv in range(1, LEVELS):
                    for d in range(2):
                        if lv > 1:
                            dve.wait_ge(*done("p_full", (u, i, d, lv - 1)))
                        off(d, lv, big_at(4096 + 512 * d, 4, P)).then_inc(*tick("noff_ready", (u, i, d, lv)))
                    gap(u, f"intra{i}", 2 + lv)
                    for d in range(2):
                        x, xt = big_at(1024 + 512 * d, 512), big_at(2048 + 512 * d, 512)
                        if lv < LEVELS - 1:
                            dve.wait_ge(*done("x_full", (u, i, d, lv)))
                            tt(x, x, pb[:, 2 + d, :], ALU.add).then_inc(*tick("x_ready", (u, i, d, lv)))
                        dve.wait_ge(*done("xt_full", (u, i, d, lv)))
                        tt(xt, xt, pb[:, 4 + d, :], ALU.add).then_inc(*tick("xt_ready", (u, i, d, lv)))
                k4 = tok[:, i, 384:640].rearrange("p (h e) -> p h e", h=4)
                v4 = tok[:, i, 640:896].rearrange("p (h e) -> p h e", h=4)
                for d in range(2):
                    b = bet[:, i, d * 4:d * 4 + 4]
                    tt(big_at(256 * d, 4, HD), v4, bc2(b, HD), ALU.mult).then_inc(*step())
                    dve.wait_ge(*stepped())
                    tt(big_at(512 + 256 * d, 4, HD), k4, bc2(b, HD), ALU.mult).then_inc(*step())
                    dve.wait_ge(*stepped())
                    last = tt(big_at(512 + 256 * d, 4, HD), big_at(512 + 256 * d, 4, HD),
                              bc2(ege[:, i, 8 + d * 4:12 + d * 4], HD), ALU.mult)
                last.then_inc(*tick("rhs_ready", (u, i)))
                gap(u, f"intra{i}", 9)
                dve.wait_ge(*done("u_copied", (u, i)))
                if g:
                    dve.wait_ge(*done("wt_copied", (u, i)))

            def gated_norm(u, i, src, gate, gain, dst, tmp, row):
                pass

            def st_scan(u):
                g, l, nt, NC, c0 = dims(u)
                h4 = "p (h e) -> p h e"
                if g:
                    for turn in range(2):
                        for d in range(2):
                            i = d if turn == 0 else 1 - d
                            k = (u, turn, d)
                            tmp = big_at(1024, 256)
                            gap(u, "scan", 2 * d if turn == 0 else 4 + d)
                            dve.wait_ge(*done("yoff_full", k))
                            e = ege[:, i, d * 4:d * 4 + 4].rearrange("p (g r) -> p g r", g=2)
                            tt(tmp.rearrange("p (g r e) -> p g r e", g=2, r=2),
                                    pb[:, 0:2, 0:P].rearrange("p g (r e) -> p g r e", r=2), bc2(e, HD), ALU.mult) \
                                        .then_inc(*tick("yoff_read", k))
                            dve.wait_ge(*done("yoff_read", k))
                            tt(ydg[:, i, :], ydg[:, i, :], tmp, ALU.add).then_inc(*step())
                            dve.wait_ge(*stepped())
                            dve.wait_ge(*done("w_full", k))
                            s4 = heads_by_parity(sol[:, i, d, :].rearrange(h4, h=4))
                            tt(s4, s4, pb[:, 2:4, 0:P].rearrange("p a (b e) -> p a b e", b=2), ALU.subtract) \
                                .then_inc(*tick("v_ready", k))
                            dve.wait_ge(*done("qs_full", k))
                            e = ege[:, i, 8 + d * 4:12 + d * 4].rearrange("p (pair par) -> p par pair", par=2)
                            tt(heads_by_parity(tmp.rearrange(h4, h=4)),
                                    pb[:, 4:6, 0:P].rearrange("p a (b e) -> p a b e", b=2), bc2(e, HD), ALU.mult) \
                                        .then_inc(*tick("qs_read", k))
                            dve.wait_ge(*done("qs_read", k))
                            if turn == 0:
                                dve.tensor_copy(og[:, i, :], tmp).then_inc(*step())
                                dve.wait_ge(*stepped())
                                gap(u, "scan", 2 * d + 1)
                                dve.wait_ge(*done("dh_full", (u, d)))
                                for h in range(4):
                                    s = slice(64 * (h // 2), 64 * (h // 2) + 64)
                                    o = h % 2 * 64
                                    last = stt(hst[s, d, o:o + 64], hst[s, d, o:o + 64], ege[s, i, 16 + d * 4 + h:17 + d * 4 + h],
                                               pb[s, 0, h * 64:h * 64 + 64], ALU.mult, ALU.add)
                                last.then_inc(*tick("h_updated", (u, d)))
                                dve.wait_ge(*done("ds_full", (u, d)))
                                for h in range(4):
                                    par, pair = h % 2, h // 2
                                    s = slice(64 * par, 64 * par + 64)
                                    c = 24 + d * 4 + h
                                    last = stt(sgd[s, d, pair, :], sgd[s, d, pair, :], ege[s, i, c:c + 1],
                                               pb[s, 2, pair * P + par * 64:pair * P + par * 64 + 64], ALU.mult, ALU.add)
                                last.then_inc(*tick("state_ready", (u, d)))
                            else:
                                tt(og[:, i, :], og[:, i, :], tmp, ALU.add).then_inc(*step())
                                dve.wait_ge(*stepped())
                gap(u, "scan", 6)
                for i in range(nt):
                    dve.wait_ge(*done("o_full", (u, i)))
                    (tt(og[:, i, :], og[:, i, :], pb[:, 2 + i, 0:256], ALU.add) if g else
                         dve.tensor_copy(og[:, i, :], pb[:, 2 + i, 0:256])).then_inc(*tick("o_read", (u, i)))
                dve.wait_ge(*done("o_read", (u, nt - 1)))
                for i in range(nt):
                    tt(ydg[:, i, :], ydg[:, i, :], zs[:, i, 0, :], ALU.mult).then_inc(*step())
                    dve.wait_ge(*stepped())
                    for m, src in enumerate((ydg, og)):
                        tmp = big_at(1280 + 256 * m, 4, HD)
                        tt(tmp, src[:, i, :].rearrange(h4, h=4), src[:, i, :].rearrange(h4, h=4), ALU.mult).then_inc(*step())
                        dve.wait_ge(*stepped())
                        last = dve.tensor_reduce(sm[:, 2 + i, 4 * m:4 * m + 4], tmp, AX_X, ALU.add)
                last.then_inc(*tick("ms_ready", u))
                gap(u, "scan", 7)
                dve.wait_ge(*done("ms_roots", u))
                dve.reciprocal(sm[:, 0:nt, :], sm[:, 0:nt, :]).then_inc(*step())
                dve.wait_ge(*stepped())
                for i in range(nt):
                    for m, src in enumerate((ydg, og)):
                        s4 = src[:, i, :].rearrange(h4, h=4)
                        y = ycat[:, i, 256 * m:256 * m + 256]
                        tt(s4, s4, bc2(sm[:, i, 4 * m:4 * m + 4], HD), ALU.mult).then_inc(*step())
                        dve.wait_ge(*stepped())
                        if m == 0:
                            tt(y, src[:, i, :], pr("sn"), ALU.mult).then_inc(*step())
                            dve.wait_ge(*stepped())
                        else:
                            tt(s4, s4, bc1(pr("gn"), 4), ALU.mult).then_inc(*step())
                            dve.wait_ge(*stepped())
                            tt(y, src[:, i, :], zs[:, i, 1, :], ALU.mult).then_inc(*step())
                            dve.wait_ge(*stepped())

            def st_attp(u):
                g, l, nt, NC, c0 = dims(u)
                dve.wait_ge(*done("fnet_full", (u, nt - 1)))
                for i in range(nt):
                    dve.wait_ge(*done("tokcols_copied", (u, 3, i)))
                    tmp = big_at(1024 + i * 384, 6, HD)
                    x6 = qkv[:, i, 0:384].rearrange("p (h e) -> p h e", h=6)
                    tt(tmp, x6, x6, ALU.mult).then_inc(*step())
                    dve.wait_ge(*stepped())
                    last = dve.tensor_reduce(sm[:, 2 + i, 0:6], tmp, AX_X, ALU.add)
                last.then_inc(*tick("att_ms", u))
                gap(u, "attp", 0)
                dve.wait_ge(*done("att_roots", u))
                dve.reciprocal(sm[:, 0:nt, 0:6], sm[:, 0:nt, 0:6]).then_inc(*step())
                dve.wait_ge(*stepped())
                for i in range(nt):
                    x6 = qkv[:, i, 0:384].rearrange("p (h e) -> p h e", h=6)
                    tmp = big_at(1024, 6, HD)
                    tt(tmp, x6, bc2(sm[:, i, 0:6], HD), ALU.mult).then_inc(*step())
                    dve.wait_ge(*stepped())
                    dst = big_at(i * 384, 384)
                    q_in = tmp[:, 0:4, :].rearrange("p (g r) e -> p g r e", g=2)
                    q_out = dst[:, 0:256].rearrange("p (r g e) -> p g r e", r=2, g=2)
                    tt(q_out, q_in, bc1(bc1(pr("qn"), 2), 2), ALU.mult).then_inc(*step())
                    dve.wait_ge(*stepped())
                    last = tt(dst[:, 256:384].rearrange("p (h e) -> p h e", h=2), tmp[:, 4:6, :], bc1(pr("kn"), 2), ALU.mult)
                    if g:
                        last.then_inc(*step())
                        dve.wait_ge(*stepped())
                        rope = con("rope").rearrange("p (i s e) -> p i s e", i=2, s=2)
                        x = dst.rearrange("p (h a e) -> p h a e", h=6, a=2)
                        tc = big_at(1536, 384).rearrange("p (h a e) -> p h a e", h=6, a=2)
                        tn = big_at(2048, 384).rearrange("p (h a e) -> p h a e", h=6, a=2)
                        tt(tc, x, bc1(bc1(rope[:, i, 0, :], 2), 6), ALU.mult).then_inc(*step())
                        dve.wait_ge(*stepped())
                        tt(tn, x, bc1(bc1(rope[:, i, 1, :], 2), 6), ALU.mult).then_inc(*step())
                        dve.wait_ge(*stepped())
                        tt(x[:, :, 0, :], tc[:, :, 0, :], tn[:, :, 1, :], ALU.subtract).then_inc(*step())
                        dve.wait_ge(*stepped())
                        last = tt(x[:, :, 1, :], tc[:, :, 1, :], tn[:, :, 0, :], ALU.add)
                    last.then_inc(*tick("qk_rows", (u, i)))

            def st_att(u, i):
                g, l, nt, NC, c0 = dims(u)
                gap(u, f"att{i}", 0)
                dve.wait_ge(*done("scores_full", (u, i)))
                s = big_at(1024, 4, 384)
                if g:
                    tt(s[:, :, 0:256], pb[:, 0:4, 0:256], bc1(con("wmask", i, 256), 4), ALU.add)
                    dve.tensor_copy(s[:, :, 256:384], pb[:, 0:4, 256:384]).then_inc(*tick("scores_read", (u, i)))
                else:
                    dve.tensor_copy(s[:, :, 0:P], pb[:, 0:4, 0:P]).then_inc(*tick("scores_read", (u, i)))
                dve.wait_ge(*done("scores_read", (u, i)))
                dve.tensor_reduce(sm[:, 3, 0:4], s[:, :, 0:384 if g else P], AX_X, ALU.max).then_inc(*step())
                dve.wait_ge(*stepped())
                stt(sm[:, 3, 0:4], sm[:, 3, 0:4], HD ** -0.5, pr("sink"), ALU.mult, ALU.max).then_inc(*step())
                dve.wait_ge(*stepped())
                ts(sm[:, 4, 0:4], sm[:, 3, 0:4], -1.0, None, ALU.mult).then_inc(*step())
                dve.wait_ge(*stepped())
                tt(sm[:, 6, 4:8], pr("sink"), sm[:, 3, 0:4], ALU.subtract).then_inc(*tick("max_ready", (u, i)))
                gap(u, f"att{i}", 1)
                dve.wait_ge(*done("sink_ready", (u, i)))
                tt(sm[:, 7, 0:4], sm[:, 5, 0:4], sm[:, 6, 0:4], ALU.add).then_inc(*step())
                dve.wait_ge(*stepped())
                dve.reciprocal(sm[:, 7, 0:4], sm[:, 7, 0:4]).then_inc(*step())
                dve.wait_ge(*stepped())
                gap(u, f"att{i}", 2)
                dve.wait_ge(*done("att_full", (u, i)))
                tt(ycat[:, i, 768:1024].rearrange("p (h e) -> p h e", h=4), pb[:, 0, 0:256].rearrange("p (h e) -> p h e", h=4),
                        bc2(sm[:, 7, 0:4], HD), ALU.mult).then_inc(*tick("att_read", (u, i)))

            def st_out(u):
                g, l, nt, NC, c0 = dims(u)
                for j in range(8):
                    gap(u, "out", j)
                    dve.wait_ge(*done("out_full", (u, j)))
                    x = xT[:, j, c0:c0 + NC]
                    stt(x, pb[:, 4 + j % 2, 0:NC], modT[:, l, 16 + j, g:g + 1], x, ALU.mult, ALU.add) \
                        .then_inc(*tick("x_added", (u, j)))

            def st_topk(u, i):
                g, l, nt, NC, c0 = dims(u)
                t = GROUP_TILES[g][i]
                for k in range(4):
                    dve.wait_ge(*done("s_copied", (u, nt - 1, k)))
                scr = (cv[:, 0:8, :].rearrange("p a b -> p (a b)") if i else dec[:, :, :, :].rearrange("p a b c -> p (a b c)"))
                scr = scr.rearrange("p (a b) -> p a b", b=P)

                points = iter(range(10))

                def top16(rows, n, vals, idx):
                    for lo in (0, 8):
                        for r in range(n):
                            last = dve.max(vals(r)[:, lo:lo + 8], rows(r))
                        last.then_inc(*step())
                        dve.wait_ge(*stepped())
                        gap(u, f"topk{i}", next(points))
                        for r in range(n):
                            last = dve.max_index(idx(r)[:, lo:lo + 8], vals(r)[:, lo:lo + 8], rows(r))
                        last.then_inc(*step())
                        dve.wait_ge(*stepped())
                        if lo == 0:
                            for r in range(n):
                                last = dve.match_replace(rows(r), vals(r)[:, 0:8], rows(r), -3.0e38)
                            last.then_inc(*step())
                            dve.wait_ge(*stepped())
                            gap(u, f"topk{i}", next(points))

                top16(lambda r: scr[:, r, :], 16, lambda r: v16[:, r, :], lambda r: i16u[:, r, :])
                dve.tensor_copy(i16f[:, :, :], i16u[:, :, :]).then_inc(*step())
                dve.wait_ge(*stepped())
                cand = attnT[:, :, :, :].rearrange("p a b c -> p (a b c)").rearrange("p (h c) -> p h c", h=8)
                v = v16[:, :, :].rearrange("p (h t) k -> p h t k", t=2)
                tt(cand.rearrange("p h (a b) -> p h a b", b=16), bc2(v[:, :, 0, :], 16),
                        v[:, :, 1, :].unsqueeze(2).to_broadcast((P, 8, 16, 16)), ALU.add).then_inc(*step())
                dve.wait_ge(*stepped())
                top16(lambda r: cand[:, r, :], 8, lambda r: best[:, r, :], lambda r: pos[:, 0, 16 * r:16 * r + 16])
                ts(pos[:, 1, :], pos[:, 0, :], 4, None, ALU.logical_shift_right).then_inc(*step())
                dve.wait_ge(*stepped())
                ts(pos[:, 2, :], pos[:, 0, :], 15, None, ALU.bitwise_and).then_inc(*step())
                dve.wait_ge(*stepped())
                dve.tensor_copy(posf[:, :, :], pos[:, 1:3, :]).then_inc(*step())
                dve.wait_ge(*stepped())
                for s in range(2):
                    gap(u, f"topk{i}", next(points))
                    eq = big_at(0, P, 16)
                    tt(eq, bc2(posf[:, s, :], 16), bc1(con("iota16"), P), ALU.is_equal).then_inc(*step())
                    dve.wait_ge(*stepped())
                    num = i16f[:, :, :].rearrange("p (h t) k -> p h t k", t=2)[:, :, s, :]
                    eq4 = big_at(0, 2048).rearrange("p (h s k) -> p h s k", h=8, s=16)
                    tt(eq4, eq4, num.unsqueeze(2).to_broadcast((P, 8, 16, 16)), ALU.mult).then_inc(*step())
                    dve.wait_ge(*stepped())
                    dve.tensor_reduce(hexp[:, s, :], eq, AX_X, ALU.add).then_inc(*step())
                    dve.wait_ge(*stepped())
                stt(idxu[:, t, :], hexp[:, 0, :], float(NKEYS), hexp[:, 1, :], ALU.mult, ALU.add) \
                    .then_inc(*tick("idx_ready", seq_tiles(u)[i][0]))
                gt = gatew[:, t, :].rearrange("p (h s) -> p h s", h=8)
                tt(gt, best[:, :, :], best[:, :, 0:1].to_broadcast((P, 8, 16)), ALU.subtract) \
                    .then_inc(*tick("best_shifted", (u, i)))
                gap(u, f"topk{i}", 9)
                dve.wait_ge(*done("gate_exp", (u, i)))
                dve.tensor_reduce(sm[:, 0, :], gt, AX_X, ALU.add).then_inc(*step())
                dve.wait_ge(*stepped())
                dve.reciprocal(sm[:, 0, :], sm[:, 0, :]).then_inc(*step())
                dve.wait_ge(*stepped())
                last = tt(gt, gt, bc2(sm[:, 0, :], 16), ALU.mult)
                if i < nt - 1:
                    last.then_inc(*step())
                    dve.wait_ge(*stepped())
                else:
                    last.then_inc(*tick("mix_done", u))

            def item_u(q, t, i0, i1, halves):
                p = phase_of["u", q]
                if i0 == 0 and 0 in halves:
                    u = [u for u in range(4) if (q, t) in seq_tiles(u)][0]
                    for k in range(2):
                        dve.wait_ge(*done("h2_copied", (u, [x for x, _ in seq_tiles(u)].index(q), k)))
                with steps(dve, i0, i1) as i:
                    for h in halves:
                        for j in range(h * HB, h * HB + HB):
                            dve.wait_ge(rows_in[j], i * 16 + 16 * (p * STEPS + 1))
                            last = dve.tensor_tensor_reduce(out=ring[:, j, :], in0=ring[:, j, :], in1=h2[:, t, :], scale=1.0,
                                                            scalar=0.0, op0=ALU.mult, op1=ALU.add, accum_out=dot8[:, j:j + 1])
                        last.then_inc(used_dve[h], 1)
                        dve.wait_ge(used_dve[h], i + (p * STEPS + 2))
                        dve.tensor_copy(dots[:, t, bass.ds(i * STEP + h * HB, HB)], dot8[:, h * HB:h * HB + HB]
                                        ).then_inc(dots_kept, 1)
                        dve.wait_ge(dots_kept, i * 2 + ((p - v_before["u", q]) * STEPS * 2 + h + 1))

            def item_gelu(q, t):
                dve.wait_ge(*done("gelu_done", q))
                if q:
                    dve.wait_ge(*done("acc_full", (q - 1, 1)))
                dve.memset(accv[:, :], 0.0)
                tt(dots[:, t, :], dots[:, t, :], gatew[:, t, :], ALU.mult).then_inc(*tick("w_ready", q))
                dve.wait_ge(*done("w_ready", q))

            def item_v(q, t, i0, i1, halves, slots):
                p = phase_of["v", q]
                own = HB - slots - 1
                base = added[0] - i0 * 2 * own - halves[0] * own
                added[0] += (i1 - i0) * len(halves) * own
                with steps(dve, i0, i1) as i:
                    for h in halves:
                        for n in range(slots, HB):
                            j = h * HB + n
                            if n > slots:
                                last.then_inc(slot_added, 1)
                                dve.wait_ge(slot_added, i * (2 * own) + (base + h * own + n - slots))
                            dve.wait_ge(rows_in[j], i * 16 + 16 * (p * STEPS + 1))
                            last = stt(accv[:, :], ring[:, j, :], dots[:, t, bass.ds(i * STEP + j, 1)], accv[:, :], ALU.mult, ALU.add)
                        last.then_inc(used_dve[h], 1)
                        dve.wait_ge(used_dve[h], i + (p * STEPS + 2))

            def item_end(u, q, t):
                g, l = UNITS[u]
                dve.wait_ge(*done("v_full", q))
                tt(accv[:, :].rearrange("p (a b) -> p a b", a=2), accv[:, :].rearrange("p (a b) -> p a b", a=2), pv[:, :, :],
                        ALU.add).then_inc(*tick("v_summed", q))
                for k in range(2):
                    dve.wait_ge(*done("acc_full", (q, k)))
                    for c in range(4):
                        j = 4 * k + c
                        x = xT[:, j, t * P:t * P + P]
                        last = stt(x, pb[:, k, c * P:c * P + P], modT[:, l, 40 + j, g:g + 1], x, ALU.mult, ALU.add)
                    last.then_inc(*tick("x_added2", (q, k)))

            stages = {"norm1": lambda u: norm(u, 0), "proj": st_proj, "scal": st_scal, "pre": st_pre,
                      "intra0": lambda u: st_intra(u, 0), "intra1": lambda u: st_intra(u, 1), "scan": st_scan,
                      "attp": st_attp, "att0": lambda u: st_att(u, 0), "att1": lambda u: st_att(u, 1),
                      "out": st_out, "query": lambda u: norm(u, 1), "topk0": lambda u: st_topk(u, 0),
                      "topk1": lambda u: st_topk(u, 1), "mod": st_mod}
            gap, run = engine_schedule({"const": item_const, "modsum": item_modsum, "u": item_u, "gelu": item_gelu,
                                        "v": item_v, "end": item_end}, stages)
            run()

    return noted


INPUTS = ["x_prompt", "x_sample", "cache_k", "cache_v", "state_ssd", "state_gdn", "c", "c_ctx", "w_mod", "b_mod",
          "norm1_w", "norm2_w", "w_in", "w_out", "ssd_conv_w", "ssd_conv_b", "ssd_A_log", "ssd_dt_bias", "ssd_D",
          "ssd_norm_w", "gdn_conv_w", "gdn_conv_b", "gdn_A_log", "gdn_dt_bias", "gdn_norm_w", "q_norm_w", "k_norm_w",
          "att_sink", "peer_w_q", "peer_keys"]
TABLES = ["peer_u", "peer_v"]
OUTPUTS = [("yp", (1, 128, D)), ("ys", (1, 256, D)), ("k", (1, DEPTH, 128, 2, HD)), ("v", (1, DEPTH, 128, 2, HD)),
           ("ssd", (1, DEPTH, 2, 4, HD, 64)), ("gdn", (1, DEPTH, 2, 4, HD, HD))]


def kernel(**inputs):
    import concourse.bacc as _bacc
    from concourse.bass_utils import run_bass_kernel_spmd as _run

    arrays = {"in_" + n: np.ascontiguousarray(inputs[n]) for n in INPUTS}
    for n in TABLES:
        for l in range(DEPTH):
            arrays[f"in_{n}{l}"] = np.ascontiguousarray(inputs[n][l])
    arrays["in_cst"], _, arrays["in_lvl"] = constants()
    seen = {}
    for _ in range(2):
        nc = _bacc.Bacc("TRN2", target_bir_lowering=False, num_devices=1)
        a, outs = {}, {}
        for name, x in arrays.items():
            a[name[3:]] = nc.dram_tensor(name, x.shape, mybir.dt.from_np(x.dtype), kind="ExternalInput").ap()
        for n, (key, shape) in enumerate(OUTPUTS):
            outs[key] = nc.dram_tensor(f"out_{n}", shape, F32, kind="ExternalOutput").ap()
        for k in "uv":
            a["tab_" + k] = [a[f"peer_{k}{l}"] for l in range(DEPTH)]
        seen = build(nc, a, outs, seen)
    r = _run(nc, [arrays], core_ids=[0])
    return tuple(r.results[0][f"out_{n}"] for n in range(len(OUTPUTS)))
```
